# Optimizing a Trainium2 kernel written in Bass

```python
import jax, jax.numpy as jnp
from jax import lax
import numpy as np

D_MODEL = 1024
BATCH = 1
SEQ = 512
DEPTH = 2

HEAD_DIM = 64
N_Q_HEADS = 12
N_KV_HEADS_A = 4
N_MEM_HEADS = 4
N_MEM = 256
MIX_WIDTH = (N_Q_HEADS + N_MEM_HEADS) * HEAD_DIM
W_IN_A = (N_Q_HEADS + 2 * N_KV_HEADS_A + N_MEM_HEADS) * HEAD_DIM
W_IN_B = (3 * N_Q_HEADS + N_MEM_HEADS) * HEAD_DIM
WINDOW = 128
BLOCK = 128
GRID_W = 64
NA_ROWS_MAX = 8
NA_COLS = 16
D_FF = -(-8 * D_MODEL // (3 * 256)) * 256
N_LAYERS_A = (DEPTH + 1) // 2
N_LAYERS_B = DEPTH // 2
EPS = 1e-6
NEG_INF = -1e30


def rmsnorm(x, g):
    x32 = x.astype(jnp.float32)
    y = x32 * lax.rsqrt(jnp.mean(x32 * x32, axis=-1, keepdims=True) + EPS)
    return (y * g.astype(jnp.float32)).astype(x.dtype)

def alibi_slopes(n_heads):
    return 2.0 ** (-8.0 * jnp.arange(1, n_heads + 1, dtype=jnp.float32) / n_heads)

def windowed_gqa(q, k, v, sink):
    B, S, H, D = q.shape
    Hk = k.shape[2]
    G = H // Hk
    nb = S // BLOCK
    qb = q.reshape(B, nb, BLOCK, Hk, G, D)
    pad = ((0, 0), (BLOCK, BLOCK), (0, 0), (0, 0))
    kp = jnp.pad(k, pad).reshape(B, nb + 2, BLOCK, Hk, D)
    vp = jnp.pad(v, pad).reshape(B, nb + 2, BLOCK, Hk, D)
    kband = jnp.concatenate([kp[:, :-2], kp[:, 1:-1], kp[:, 2:]], axis=2)
    vband = jnp.concatenate([vp[:, :-2], vp[:, 1:-1], vp[:, 2:]], axis=2)
    q_pos = jnp.arange(S).reshape(nb, BLOCK)
    k_pos = jnp.arange(nb)[:, None] * BLOCK - BLOCK + jnp.arange(3 * BLOCK)[None, :]
    dist = jnp.abs(q_pos[:, :, None] - k_pos[:, None, :])
    allowed = (dist <= WINDOW) & (k_pos[:, None, :] >= 0) & (k_pos[:, None, :] < S)
    slopes = alibi_slopes(H).reshape(1, Hk, G, 1, 1, 1)
    s = jnp.einsum('bnikgd,bnukd->bkgniu', qb, kband).astype(jnp.float32) * (D ** -0.5)
    s = s - slopes * dist.astype(jnp.float32)[None, None, None]
    s = jnp.where(allowed[None, None, None], s, NEG_INF)
    sink_col = jnp.broadcast_to(sink.astype(jnp.float32).reshape(1, Hk, G, 1, 1, 1), s.shape[:-1] + (1,))
    p = jax.nn.softmax(jnp.concatenate([s, sink_col], axis=-1), axis=-1)[..., :-1]
    o = jnp.einsum('bkgniu,bnukd->bnikgd', p.astype(v.dtype), vband)
    return o.reshape(B, S, H * D)

def neighbourhood_attn(q, k, v, rpb):
    B, S, H, D = q.shape
    rows = S // GRID_W
    kr = min(NA_ROWS_MAX, rows)
    qg = q.reshape(B, rows, GRID_W, H, D)
    kg = k.reshape(B, rows, GRID_W, H, D)
    vg = v.reshape(B, rows, GRID_W, H, D)
    r = jnp.arange(rows)
    row_start = jnp.clip(r - kr // 2, 0, rows - kr)
    row_idx = row_start[:, None] + jnp.arange(kr)[None, :]
    kband = kg[:, row_idx]
    vband = vg[:, row_idx]
    c = jnp.arange(GRID_W)
    col_start = jnp.clip(c - NA_COLS // 2, 0, GRID_W - NA_COLS)
    in_win = (c[None, :] >= col_start[:, None]) & (c[None, :] < col_start[:, None] + NA_COLS)
    dr_idx = row_idx - r[:, None] + NA_ROWS_MAX - 1
    dc_idx = jnp.clip(c[None, :] - c[:, None], -(NA_COLS - 1), NA_COLS - 1) + NA_COLS - 1
    bias = rpb.astype(jnp.float32)[:, dr_idx][:, :, :, dc_idx]
    bias = bias.transpose(0, 1, 3, 2, 4)
    s = jnp.einsum('brchd,brijhd->bhrcij', qg, kband).astype(jnp.float32) * (D ** -0.5)
    s = s + bias[None]
    s = jnp.where(in_win[None, None, None, :, None, :], s, NEG_INF)
    sh = s.shape
    p = jax.nn.softmax(s.reshape(sh[:-2] + (kr * GRID_W,)), axis=-1).reshape(sh)
    o = jnp.einsum('bhrcij,brijhd->brchd', p.astype(v.dtype), vband)
    return o.reshape(B, S, H * D)

def memory_attn(q, k, v):
    B, S, Hm, D = q.shape
    s = jnp.einsum('bshd,bmhd->bhsm', q, k).astype(jnp.float32) * (D ** -0.5)
    p = jax.nn.softmax(s, axis=-1)
    o = jnp.einsum('bhsm,bmhd->bshd', p.astype(v.dtype), v)
    return o.reshape(B, S, Hm * D)

def first_inputs(seed: int = 0) -> dict:
    key = jax.random.key(seed)
    ks = jax.random.split(key, 16)
    f32 = jnp.float32
    nrm = lambda k, shape, scale: jax.random.normal(k, shape, f32) * scale
    return {
        "x": nrm(ks[0], (BATCH, SEQ, D_MODEL), 1.0),
        "mem": nrm(ks[1], (BATCH, N_MEM, D_MODEL), 1.0),
        "norm_mix": 1.0 + nrm(ks[2], (DEPTH, D_MODEL), 0.02),
        "norm_ffn": 1.0 + nrm(ks[3], (DEPTH, D_MODEL), 0.02),
        "norm_mem": 1.0 + nrm(ks[4], (D_MODEL,), 0.02),
        "norm_final": 1.0 + nrm(ks[5], (D_MODEL,), 0.02),
        "w_in_a": nrm(ks[6], (N_LAYERS_A, D_MODEL, W_IN_A), D_MODEL ** -0.5),
        "sink_a": nrm(ks[7], (N_LAYERS_A, N_Q_HEADS), 0.5),
        "w_in_b": nrm(ks[8], (N_LAYERS_B, D_MODEL, W_IN_B), D_MODEL ** -0.5),
        "rpb_b": nrm(ks[9], (N_LAYERS_B, N_Q_HEADS, 2 * NA_ROWS_MAX - 1, 2 * NA_COLS - 1), 0.3),
        "w_mem_kv": nrm(ks[10], (DEPTH, D_MODEL, 2 * N_MEM_HEADS * HEAD_DIM), D_MODEL ** -0.5),
        "w_out": nrm(ks[11], (DEPTH, MIX_WIDTH, D_MODEL), MIX_WIDTH ** -0.5),
        "w_gate_up": nrm(ks[12], (DEPTH, D_MODEL, 2 * D_FF), D_MODEL ** -0.5),
        "w_down": nrm(ks[13], (DEPTH, D_FF, D_MODEL), D_FF ** -0.5),
    }

def first_block(x, mem, norm_mix, norm_ffn, norm_mem, norm_final, w_in_a, sink_a, w_in_b, rpb_b,
              w_mem_kv, w_out, w_gate_up, w_down):
    B, S, _ = x.shape
    qw = N_Q_HEADS * HEAD_DIM
    kvw = N_KV_HEADS_A * HEAD_DIM
    mw = N_MEM_HEADS * HEAD_DIM
    mem_n = rmsnorm(mem, norm_mem)
    for i in range(DEPTH):
        li = i // 2
        h = rmsnorm(x, norm_mix[i])
        mkv = mem_n @ w_mem_kv[i]
        mk = mkv[..., :mw].reshape(B, N_MEM, N_MEM_HEADS, HEAD_DIM)
        mv = mkv[..., mw:].reshape(B, N_MEM, N_MEM_HEADS, HEAD_DIM)
        if i % 2 == 0:
            proj = h @ w_in_a[li]
            q, k, v, qm = jnp.split(proj, [qw, qw + kvw, qw + 2 * kvw], axis=-1)
            y_tok = windowed_gqa(q.reshape(B, S, N_Q_HEADS, HEAD_DIM),
                                 k.reshape(B, S, N_KV_HEADS_A, HEAD_DIM),
                                 v.reshape(B, S, N_KV_HEADS_A, HEAD_DIM), sink_a[li])
        else:
            proj = h @ w_in_b[li]
            q, k, v, qm = jnp.split(proj, [qw, 2 * qw, 3 * qw], axis=-1)
            y_tok = neighbourhood_attn(q.reshape(B, S, N_Q_HEADS, HEAD_DIM),
                                       k.reshape(B, S, N_Q_HEADS, HEAD_DIM),
                                       v.reshape(B, S, N_Q_HEADS, HEAD_DIM), rpb_b[li])
        y_mem = memory_attn(qm.reshape(B, S, N_MEM_HEADS, HEAD_DIM), mk, mv)
        x = x + jnp.concatenate([y_tok, y_mem], axis=-1) @ w_out[i]
        h = rmsnorm(x, norm_ffn[i])
        gu = h @ w_gate_up[i]
        x = x + (jax.nn.silu(gu[..., :D_FF]) * gu[..., D_FF:]) @ w_down[i]
    return rmsnorm(x, norm_final)


N_META = 16
D_CONV = 512
CONV_A_WIDTH = 3
DN_HEADS = 4
DN_HEAD_DIM = 128
DN_DIM = DN_HEADS * DN_HEAD_DIM
DN_CONV_WIDTH = 4
DN_CHUNK = 64
D_MIX = D_CONV + DN_DIM
IN_DIM = 3 * D_CONV + 4 * DN_DIM + 2 * DN_HEADS
SWA_HEADS = 16
SWA_KV_HEADS = 4
SWA_HEAD_DIM = 64
SWA_WINDOW = 128
SWA_BLOCK = 128
D_FF_2 = 2816
FFN_CONV_WIDTH = 3
N_EVEN = (DEPTH + 1) // 2
N_ODD = DEPTH // 2


def rms_norm(x, w):
    xf = x.astype(jnp.float32)
    y = xf * lax.rsqrt(jnp.mean(xf * xf, -1, keepdims=True) + EPS)
    return (y * w.astype(jnp.float32)).astype(x.dtype)

def l2_norm(x):
    return x * lax.rsqrt(jnp.sum(x * x, -1, keepdims=True) + EPS)

def causal_dwconv(x, w):
    k = w.shape[0]
    return lax.conv_general_dilated(
        x, w[:, None, :].astype(x.dtype), window_strides=(1,), padding=((k - 1, 0),),
        dimension_numbers=('NWC', 'WIO', 'NWC'), feature_group_count=x.shape[-1])

def gated_delta_rule(q, k, v, beta, g):
    q, k, v, beta, g = (t.astype(jnp.float32) for t in (q, k, v, beta, g))
    b, l, h, dk = q.shape
    dv = v.shape[-1]
    c = DN_CHUNK
    n = l // c

    def chunks(t):
        t = t.reshape((b, n, c, h) + t.shape[3:])
        return jnp.moveaxis(t, 3, 1)

    q, k, v, beta, g = chunks(q), chunks(k), chunks(v), chunks(beta), chunks(g)
    decay = jnp.cumsum(g, -1)
    diff = decay[..., :, None] - decay[..., None, :]
    idx = jnp.arange(c)
    strict = idx[:, None] > idx[None, :]
    incl = idx[:, None] >= idx[None, :]
    dmask = jnp.exp(jnp.where(incl, diff, -jnp.inf))
    kk = jnp.einsum('bhnid,bhnjd->bhnij', k, k)
    a_strict = jnp.where(strict, beta[..., None] * kk * dmask, 0.0)
    t_mat = a_strict + jnp.eye(c, dtype=jnp.float32)
    rhs = jnp.concatenate([v * beta[..., None], k * (beta * jnp.exp(decay))[..., None]], -1)
    sol = lax.linalg.triangular_solve(t_mat, rhs, left_side=True, lower=True, unit_diagonal=True)
    u = sol[..., :dv]
    w = sol[..., dv:]
    qk = jnp.einsum('bhnid,bhnjd->bhnij', q, k) * dmask
    q_dec = q * jnp.exp(decay)[..., None]
    k_dec = k * jnp.exp(decay[..., -1:] - decay)[..., None]
    g_last = jnp.exp(decay[..., -1])

    def step(s, inp):
        u_n, w_n, qk_n, qd_n, kd_n, gl_n = inp
        v_new = u_n - jnp.einsum('bhcd,bhde->bhce', w_n, s)
        o = jnp.einsum('bhcd,bhde->bhce', qd_n, s) + jnp.einsum('bhij,bhje->bhie', qk_n, v_new)
        s = s * gl_n[..., None, None] + jnp.einsum('bhcd,bhce->bhde', kd_n, v_new)
        return s, o

    xs = tuple(jnp.moveaxis(t, 2, 0) for t in (u, w, qk, q_dec, k_dec, g_last))
    s0 = jnp.zeros((b, h, dk, dv), jnp.float32)
    _, o = lax.scan(step, s0, xs)
    return jnp.transpose(o, (1, 0, 3, 2, 4)).reshape(b, l, h, dv)

def even_mixer(h, w_in, conv_a_w, dn_conv_w, a_log, dt_bias, dn_norm_w, w_out):
    b, l, _ = h.shape
    p = h @ w_in
    sizes = [D_CONV, D_CONV, D_CONV, 3 * DN_DIM, DN_DIM, DN_HEADS, DN_HEADS]
    splits = [sum(sizes[:i + 1]) for i in range(len(sizes) - 1)]
    a_gate_in, a_gate_out, a_h, qkv, z, beta_raw, alpha_raw = jnp.split(p, splits, -1)
    y_a = a_gate_out * causal_dwconv(a_gate_in * a_h, conv_a_w)
    qkv = jax.nn.silu(causal_dwconv(qkv, dn_conv_w))
    q, k, v = jnp.split(qkv, 3, -1)
    hd = (b, l, DN_HEADS, DN_HEAD_DIM)
    q = l2_norm(q.reshape(hd).astype(jnp.float32)) * (DN_HEAD_DIM ** -0.5)
    k = l2_norm(k.reshape(hd).astype(jnp.float32))
    v = v.reshape(hd).astype(jnp.float32)
    beta = jax.nn.sigmoid(beta_raw.astype(jnp.float32))
    g = -jnp.exp(a_log.astype(jnp.float32)) * jax.nn.softplus(
        alpha_raw.astype(jnp.float32) + dt_bias.astype(jnp.float32))
    pad = (-N_META) % DN_CHUNK
    padw = lambda t: jnp.pad(t, ((0, 0), (pad, 0)) + ((0, 0),) * (t.ndim - 2))
    o = gated_delta_rule(padw(q), padw(k), padw(v), padw(beta), padw(g))[:, pad:]
    o = rms_norm(o, dn_norm_w) * jax.nn.silu(z.reshape(hd).astype(jnp.float32))
    y_b = o.reshape(b, l, DN_DIM).astype(h.dtype)
    return jnp.concatenate([y_a, y_b], -1) @ w_out

def sink_softmax(logits, sink):
    m = jnp.maximum(jnp.max(logits, -1, keepdims=True), sink)
    e = jnp.exp(logits - m)
    return e / (jnp.sum(e, -1, keepdims=True) + jnp.exp(sink - m))

def swa_mixer(h, wq, wk, wv, q_norm_w, k_norm_w, sinks, wo):
    b, l, _ = h.shape
    kv, grp, d = SWA_KV_HEADS, SWA_HEADS // SWA_KV_HEADS, SWA_HEAD_DIM
    q = rms_norm((h @ wq).reshape(b, l, kv, grp, d), q_norm_w) * (d ** -0.5)
    k = rms_norm((h @ wk).reshape(b, l, kv, d), k_norm_w)
    v = (h @ wv).reshape(b, l, kv, d)
    sink = sinks.astype(jnp.float32).reshape(kv, grp)
    qm, qr = q[:, :N_META], q[:, N_META:]
    km, kr = k[:, :N_META], k[:, N_META:]
    vm, vr = v[:, :N_META], v[:, N_META:]
    sm = jnp.einsum('bikgd,bjkd->bkgij', qm, km).astype(jnp.float32)
    mmask = jnp.tril(jnp.ones((N_META, N_META), bool))
    pm = sink_softmax(jnp.where(mmask, sm, -jnp.inf), sink[None, :, :, None, None])
    om = jnp.einsum('bkgij,bjkd->bikgd', pm.astype(v.dtype), vm).reshape(b, N_META, SWA_HEADS * d)
    s_real = l - N_META
    nb = s_real // SWA_BLOCK
    qb = qr.reshape(b, nb, SWA_BLOCK, kv, grp, d)
    kb = kr.reshape(b, nb, SWA_BLOCK, kv, d)
    vb = vr.reshape(b, nb, SWA_BLOCK, kv, d)
    band = lambda t: jnp.concatenate(
        [jnp.concatenate([jnp.zeros_like(t[:, :1]), t[:, :-1]], 1), t], 2)
    kband, vband = band(kb), band(vb)
    s_meta = jnp.einsum('bnikgd,bjkd->bnkgij', qb, km).astype(jnp.float32)
    s_band = jnp.einsum('bnikgd,bnjkd->bnkgij', qb, kband).astype(jnp.float32)
    i = jnp.arange(SWA_BLOCK)[:, None]
    j = jnp.arange(2 * SWA_BLOCK)[None, :]
    n = jnp.arange(nb)[:, None, None]
    rel = i + SWA_BLOCK - j
    valid = (rel >= 0) & (rel < SWA_WINDOW) & (n * SWA_BLOCK - SWA_BLOCK + j >= 0)
    s_band = jnp.where(valid[None, :, None, None], s_band, -jnp.inf)
    p = sink_softmax(jnp.concatenate([s_meta, s_band], -1), sink[None, None, :, :, None, None])
    p = p.astype(v.dtype)
    orr = (jnp.einsum('bnkgim,bmkd->bnikgd', p[..., :N_META], vm)
           + jnp.einsum('bnkgij,bnjkd->bnikgd', p[..., N_META:], vband))
    orr = orr.reshape(b, s_real, SWA_HEADS * d)
    return jnp.concatenate([om, orr], 1) @ wo

def conv_ffn(h, w_up, conv_w, w_down):
    gate, val = jnp.split(h @ w_up, 2, -1)
    gate = causal_dwconv(gate, conv_w)
    return (jax.nn.silu(gate) * val) @ w_down

def second_inputs(seed: int = 0) -> dict:
    key = jax.random.key(seed)
    ks = jax.random.split(key, 24)
    nrm = lambda k, s, scale: jax.random.normal(k, s, jnp.float32) * scale
    gain = lambda k, s: 1.0 + 0.05 * jax.random.normal(k, s, jnp.float32)
    dt = jnp.exp(jax.random.uniform(ks[7], (N_EVEN, DN_HEADS), jnp.float32, np.log(1e-3), np.log(1e-1)))
    return {
        "x": nrm(ks[0], (BATCH, SEQ, D_MODEL), 1.0),
        "meta_tokens": nrm(ks[1], (N_META, D_MODEL), 1.0),
        "attn_norm_w": gain(ks[2], (DEPTH, D_MODEL)),
        "ffn_norm_w": gain(ks[3], (DEPTH, D_MODEL)),
        "mix_w_in": nrm(ks[4], (N_EVEN, D_MODEL, IN_DIM), D_MODEL ** -0.5),
        "conv_a_w": nrm(ks[5], (N_EVEN, CONV_A_WIDTH, D_CONV), CONV_A_WIDTH ** -0.5),
        "dn_conv_w": nrm(ks[6], (N_EVEN, DN_CONV_WIDTH, 3 * DN_DIM), DN_CONV_WIDTH ** -0.5),
        "dn_a_log": jnp.log(jax.random.uniform(ks[8], (N_EVEN, DN_HEADS), jnp.float32, 1.0, 16.0)),
        "dn_dt_bias": dt + jnp.log(-jnp.expm1(-dt)),
        "dn_norm_w": gain(ks[9], (N_EVEN, DN_HEAD_DIM)),
        "mix_w_out": nrm(ks[10], (N_EVEN, D_MIX, D_MODEL), D_MIX ** -0.5),
        "swa_wq": nrm(ks[11], (N_ODD, D_MODEL, SWA_HEADS * SWA_HEAD_DIM), D_MODEL ** -0.5),
        "swa_wk": nrm(ks[12], (N_ODD, D_MODEL, SWA_KV_HEADS * SWA_HEAD_DIM), D_MODEL ** -0.5),
        "swa_wv": nrm(ks[13], (N_ODD, D_MODEL, SWA_KV_HEADS * SWA_HEAD_DIM), D_MODEL ** -0.5),
        "swa_q_norm_w": gain(ks[14], (N_ODD, SWA_HEAD_DIM)),
        "swa_k_norm_w": gain(ks[15], (N_ODD, SWA_HEAD_DIM)),
        "swa_sinks": nrm(ks[16], (N_ODD, SWA_HEADS), 0.5),
        "swa_wo": nrm(ks[17], (N_ODD, SWA_HEADS * SWA_HEAD_DIM, D_MODEL), (SWA_HEADS * SWA_HEAD_DIM) ** -0.5),
        "ffn_w_up": nrm(ks[18], (DEPTH, D_MODEL, 2 * D_FF_2), D_MODEL ** -0.5),
        "ffn_conv_w": nrm(ks[19], (DEPTH, FFN_CONV_WIDTH, D_FF_2), FFN_CONV_WIDTH ** -0.5),
        "ffn_w_down": nrm(ks[20], (DEPTH, D_FF_2, D_MODEL), D_FF_2 ** -0.5),
    }

def second_block(x, meta_tokens, attn_norm_w, ffn_norm_w, mix_w_in, conv_a_w, dn_conv_w, dn_a_log,
              dn_dt_bias, dn_norm_w, mix_w_out, swa_wq, swa_wk, swa_wv, swa_q_norm_w, swa_k_norm_w,
              swa_sinks, swa_wo, ffn_w_up, ffn_conv_w, ffn_w_down):
    b = x.shape[0]
    meta = jnp.broadcast_to(meta_tokens[None].astype(x.dtype), (b, N_META, D_MODEL))
    h = jnp.concatenate([meta, x], 1)
    for layer in range(DEPTH):
        i = layer // 2
        hn = rms_norm(h, attn_norm_w[layer])
        if layer % 2 == 0:
            mix = even_mixer(hn, mix_w_in[i], conv_a_w[i], dn_conv_w[i], dn_a_log[i],
                             dn_dt_bias[i], dn_norm_w[i], mix_w_out[i])
        else:
            mix = swa_mixer(hn, swa_wq[i], swa_wk[i], swa_wv[i], swa_q_norm_w[i],
                            swa_k_norm_w[i], swa_sinks[i], swa_wo[i])
        h = h + mix.astype(h.dtype)
        ff = conv_ffn(rms_norm(h, ffn_norm_w[layer]), ffn_w_up[layer], ffn_conv_w[layer], ffn_w_down[layer])
        h = h + ff.astype(h.dtype)
    return h[:, N_META:]


def setup_inputs(seed=0):
    out = dict(first_inputs(seed))
    for name, value in second_inputs(seed + 1).items():
        if name != "x":
            out[name + "_2"] = value
    return out


def reference(
    x, mem, norm_mix, norm_ffn, norm_mem, norm_final, w_in_a, sink_a, w_in_b, rpb_b, w_mem_kv,
    w_out, w_gate_up, w_down, meta_tokens_2, attn_norm_w_2, ffn_norm_w_2, mix_w_in_2,
    conv_a_w_2, dn_conv_w_2, dn_a_log_2, dn_dt_bias_2, dn_norm_w_2, mix_w_out_2, swa_wq_2,
    swa_wk_2, swa_wv_2, swa_q_norm_w_2, swa_k_norm_w_2, swa_sinks_2, swa_wo_2, ffn_w_up_2,
    ffn_conv_w_2, ffn_w_down_2,
):
    x = first_block(
        x, mem, norm_mix, norm_ffn, norm_mem, norm_final, w_in_a, sink_a, w_in_b, rpb_b,
        w_mem_kv, w_out, w_gate_up, w_down,
    )
    return second_block(
        x, meta_tokens_2, attn_norm_w_2, ffn_norm_w_2, mix_w_in_2, conv_a_w_2, dn_conv_w_2,
        dn_a_log_2, dn_dt_bias_2, dn_norm_w_2, mix_w_out_2, swa_wq_2, swa_wk_2, swa_wv_2,
        swa_q_norm_w_2, swa_k_norm_w_2, swa_sinks_2, swa_wo_2, ffn_w_up_2, ffn_conv_w_2,
        ffn_w_down_2,
    )


_drawn_inputs = setup_inputs


def setup_inputs(seed=0):
    import zlib

    import numpy as np

    out = dict(_drawn_inputs(seed))
    spreads = {}
    factors = {'norm_mix': 3.776,
     'norm_mem': 8.0,
     'sink_a': 78.351,
     'dn_norm_w_2': 3.446,
     'swa_q_norm_w_2': 8.0,
     'swa_k_norm_w_2': 8.0,
     'swa_sinks_2': 8.0}
    for name, (base, spread) in spreads.items():
        noise = np.random.default_rng([zlib.crc32(name.encode()), seed]).standard_normal(out[name].shape)
        drawn = base * np.exp(spread * noise) if base else spread * noise
        out[name] = __import__('jax').numpy.asarray(drawn.astype(out[name].dtype))
    for name, factor in factors.items():
        out[name] = (out[name] * factor).astype(out[name].dtype)
    return out
```

```python
import math
from contextlib import ExitStack, contextmanager

import concourse.bass as bass
from concourse import mybir

P = 128
D = 1024
DT = D // P
META = 16
SEQ = 512
TOK = META + SEQ
HALF = TOK // 2
MEM = 256
HD = 64
FF_T = 2816 // P
FF_G = 2
FF_J = FF_T // FF_G
UP, DOWN = DT, FF_J
EPS = 1e-6
NEG = -1e30
RING = 2
BANK = 512
KEY_STEP = P + META
N_NORM = 10
L0_PAIRS = [(0, 3), (1, 4), (2, 5), (6, 9), (7, 10), (8, 11)]
L3_PAIRS = [(0, 4), (1, 5), (2, 6), (3, 7), (8, 12), (9, 13), (10, 14), (11, 15)]
RPB_R, RPB_C, GRID = 15, 31, 64
RPB_W = 2 * GRID - 1
DN_H = 4
LEVELS = 7


class Stage:

    def __init__(self, kind, slab0, norm0, nh0, pair0, tile0, tn0, ffn0, blk=None, src=None, gain=None, after=None,
                 nf=None, nv=None, nt=None, blocks=None, bias=None, sink=None, qt=None, kt=None, group=None, y=None,
                 layer=None, conv=None, y2=None, what=None, n=None):
        self.kind, self.blk, self.layer = kind, blk, layer
        self.slab0, self.norm0, self.nh0, self.pair0 = slab0, norm0, nh0, pair0
        self.tile0, self.tn0, self.ffn0 = tile0, tn0, ffn0
        self.src, self.gain, self.after = src, gain, after
        self.nf, self.nv = nf, nv
        self.nt, self.blocks, self.bias, self.sink = nt, blocks, bias, sink
        self.qt, self.kt, self.group, self.y = qt, kt, group, y
        self.conv, self.y2, self.what, self.n = conv, y2, what, n
        self.next_norm = None


def plan():
    out = []
    c = dict(slab=0, norm=0, nh=0, pair=0, tile=0, tn=0, ffn=0)
    kinds = []

    def slabs(n, size):
        kinds.extend([size] * n)
        c["slab"] += n

    def add(kind, **kw):
        out.append(Stage(kind, **{k + "0": v for k, v in c.items()}, **kw))
        return out[-1]

    def norm(src, gain, blk):
        after = "loads" if gain <= 1 else "final" if gain == 6 else "slabs"
        s = add("norm", src=src, gain=gain, blk=blk, after=after)
        c["norm"] += 1
        if src != "final":
            c["nh"] += 1
        return s

    def proj(nf, nv, blk):
        add("proj", nf=nf, nv=nv, blk=blk)
        slabs(nf + nv, UP)

    def att(**kw):
        s = add("att", **kw)
        c["pair"] += kw["nt"] * len(kw["blocks"])
        c["tile"] += kw["nt"]

    def tail(gain, blk, layer, conv):
        add("out", blk=blk, y2=conv and layer == 0)
        slabs(DT, UP)
        norm("x", gain, blk)
        add("ffn", blk=blk, layer=layer, conv=conv)
        for _ in range(FF_G):
            slabs(2 * FF_J, UP)
            slabs(DT, DOWN)
        c["ffn"] += 1

    norm("mem", 0, 0)
    add("memkv")
    slabs(8, UP)
    a_blocks = [dict(q=META + P * b, nq=P, keys=[(META + P * max(b - 1, 0), P * (min(b + 1, 3) - max(b - 1, 0) + 1))],
                     chunks=[(P * i, P, max(b - 1, 0) + i) for i in range(min(b + 1, 3) - max(b - 1, 0) + 1)],
                     bias=P if b == 0 else 0) for b in range(4)]
    n_blocks = [dict(q=META + P * b, nq=P, keys=[(META, SEQ)], chunks=[(P * i, P, i) for i in range(4)],
                     bias=(RPB_R // 2 - 1 - 2 * b) * GRID) for b in range(4)]
    m_blocks = [dict(q=META + P * b, nq=P, keys=[(0, MEM)], chunks=[(P * i, P, i) for i in range(2)], bias=0)
                for b in range(4)]
    s_blocks = [dict(q=0, nq=META, keys=[(P, META)], chunks=[(0, META, 4)], bias="meta"),
                dict(q=META, nq=P, keys=[(0, KEY_STEP)], chunks=[(0, P, 0), (P, META, 4)], bias="first")]
    for b in range(1, 4):
        s_blocks.append(dict(q=META + P * b, nq=P, keys=[(KEY_STEP * (b - 1), P + KEY_STEP)],
                             chunks=[(0, P, b - 1), (KEY_STEP, P, b), (P, META, 4)], bias="band"))
    norm("x", 1, 1)
    proj(10, 2, 1)
    att(nt=6, blocks=a_blocks, bias="alibi", sink=0, qt=0, kt=6, group=3, y=0, layer=0)
    att(nt=2, blocks=m_blocks, bias=None, sink=None, qt=8, kt=0, group=1, y=6, layer=0)
    tail(2, 1, 0, False)
    norm("x", 3, 1)
    proj(14, 6, 1)
    att(nt=6, blocks=n_blocks, bias="rpb", sink=None, qt=0, kt=6, group=1, y=0, layer=1)
    att(nt=2, blocks=m_blocks, bias=None, sink=None, qt=12, kt=0, group=1, y=6, layer=1)
    tail(4, 1, 1, False)
    norm("final", 5, 1)
    norm("x", 6, 2)
    add("even")
    slabs(28, UP)
    add("tn", what="l2", n=8)
    c["tn"] += 8
    add("delta")
    add("tn", what="head", n=4)
    c["tn"] += 4
    tail(7, 2, 0, True)
    norm("x", 8, 2)
    proj(10, 2, 2)
    add("tn", what="qk", n=10)
    c["tn"] += 10
    att(nt=8, blocks=s_blocks, bias="band", sink=1, qt=0, kt=8, group=4, y=0, layer=3)
    tail(9, 2, 1, True)
    for a, b in zip(out, out[1:]):
        if b.kind == "norm" and b.after == "slabs":
            a.next_norm = b
    return out, kinds


def delta_steps(n):
    levels = [s for s in range(1, LEVELS) if (1 << s) < n]
    pe = ["rows", "kk", "kq", "at"]
    dve = ["kc", "vc", "gb", "row", "dcol", "dlast", "dt", "dtm", "dl", "dlm", "a1", "a", "qk", "at",
           "x1", "x", "xt1", "xt"]
    pool = [("am", s) for s in levels]
    act = ["erow", "edec", "elast", "edt", "edl"]
    for s in levels:
        pe += [("z", s)] + [("xx", s)] * (s != levels[-1]) + [("xz", s)]
        dve += [("x", s)] * (s != levels[-1]) + [("xt", s)]
        act += [("z", s)]
    pe += ["vt", "ks", "kt", "vn", "o", "s"]
    dve += ["bed", "r1", "r2", "r", "kd", "qd", "s1", "s", "o"]
    act += ["vn"]
    return levels, pe, dve, act, pool


def build(nc, d):
    f32, f32r = mybir.dt.float32, mybir.dt.float32r
    ALU, ACT, AX = mybir.AluOpType, mybir.ActivationFunctionType, mybir.AxisListType
    stages, kinds = plan()
    n_slabs = len(kinds)

    ctx = ExitStack()
    with ctx:
        def sb(name, shape, dt=f32):
            return ctx.enter_context(nc.sbuf_tensor(name, shape, dt))

        def sem(name):
            return ctx.enter_context(nc.semaphore(name))

        x = sb("x", [P, DT, TOK])
        h_hi = sb("h_hi", [P, DT, TOK], f32r)
        h_lo = sb("h_lo", [P, DT, TOK], f32r)
        raw = sb("raw", [P, RING, DOWN * P])
        w_hi = sb("w_hi", [P, RING, DOWN * P], f32r)
        w_lo = sb("w_lo", [P, RING, DOWN * P], f32r)
        cst = sb("cst", [P, d["consts"].shape[1]])
        ident, ones, halves, tri = (cst[:, i * P:(i + 1) * P] for i in range(4))
        o = 4 * P
        grid_mask = cst[:, o:o + GRID]
        band_mask = cst[:, o + GRID:o + GRID + 2 * P + META]
        first_mask = cst[:, o + GRID + 2 * P + META:o + GRID + 3 * P + 2 * META]
        meta_mask = cst[0:META, o + GRID + 3 * P + 2 * META:o + GRID + 3 * P + 3 * META]
        vec = sb("vec", [P, d["vectors"].shape[1]])
        gains = vec[:, 0:N_NORM * DT].rearrange("p (n m) -> p n m", n=N_NORM)
        o = N_NORM * DT
        ffn_taps = vec[:, o:o + 2 * FF_T * 3].rearrange("p (l j k) -> p l j k", l=2, k=3)
        o += 2 * FF_T * 3
        a_taps = vec[:, o:o + 12].rearrange("p (j k) -> p j k", k=3)
        dn_taps = vec[:, o + 12:o + 60].rearrange("p (j k) -> p j k", k=4)
        dn_gain, q_gain, k_gain, eps_col = (vec[:, o + 60 + i:o + 61 + i] for i in range(4))
        rows = sb("rows", [P, 12 + 16 + 8])
        sinks = [rows[:, 0:12], rows[:, 12:28]]
        a_log, dt_bias = rows[:, 28:32], rows[:, 32:36]
        sq_sum = sb("sq_sum", [P, TOK])
        mk = sb("mk", [P, 2, 2, MEM])
        mv = sb("mv", [P, 2, 2, 2 * P])

        def region(name, words):
            at = nc.sbuf_base
            sb(name, [P, words])
            used = [0]

            def place(tag, shape, dt=f32, at_word=None):
                if at_word is not None:
                    used[0] = at_word
                size = math.prod(shape[1:])
                t = nc.alloc_sbuf_tensor_at(tag, shape, dt, offset=at + 4 * used[0])
                used[0] += (size + 7) // 8 * 8
                assert used[0] <= words, (tag, used[0])
                return t
            return place

        big = region("big", 2 * FF_J * TOK)
        small = region("small", 13024)
        act_hi = big("act_hi", [P, FF_J, TOK], f32r, 0)
        act_lo = big("act_lo", [P, FF_J, TOK], f32r)
        mem_in = big("mem_in", [P, DT, MEM], f32, 0)
        qk = big("qk", [P, 14, TOK], f32, 0)
        val = big("val", [P, 5, 6 * P])
        qkv = big("qkv", [P, 12, TOK], f32, 0)
        zed = big("zed", [P, DN_H, TOK])
        conv_y = big("conv_y", [P, 4, TOK])
        bias_sb = small("bias_sb", [P, 2, 2, (RPB_R - 1) * GRID], f32, 0)
        s_sb = small("s_sb", [P, 2, 2, 514])
        p_t = small("p_t", [P, 2, 4, P])
        y_sb = small("y_sb", [P, 2, P])
        n_max = small("n_max", [P, 2, 2])
        p_sum = small("p_sum", [P, 2, 2])
        p_inv = small("p_inv", [P, 2, 2])
        p_rec = small("p_rec", [P, 2, P])
        q_hi, q_lo = (small(n, [P, 2, TOK], f32r) for n in ("q_hi", "q_lo"))
        k_hi, k_lo = (small(n, [P, 2, 4 * KEY_STEP], f32r) for n in ("k_hi", "k_lo"))
        v_st = small("v_st", [P, 2, 5, P])
        sq = small("sq", [P, 2, TOK], f32, 4096)
        rstd = small("rstd", [P, TOK])
        normed = small("normed", [P, 2, TOK])
        silu_g = small("silu_g", [P, TOK], f32, 4096)
        prod = small("prod", [P, TOK])
        padded = small("padded", [P, 2, 3 + TOK])
        conv = small("conv", [P, 2, TOK])
        root = small("root", [P, 2, TOK], f32, 4096 + 2 * TOK)
        normed_o = small("normed_o", [P, 2, TOK])
        four = [P, DN_H, P]
        kc, vc, gb, row, dt_, dl_, a_m, a_t, x_m, x_t, z_m, res = (
            small(n, four, f32, 0 if n == "kc" else None)
            for n in ("kc", "vc", "gb", "row", "dt_", "dl_", "a_m", "a_t", "x_m", "x_t", "z_m", "res"))
        erow, qk_t, state = (small(n, four) for n in ("erow", "qk_t", "state"))
        r1, v_new, k_dec, q_dec = z_m, x_m, a_m, a_t
        a_lv = small("a_lv", [P, 2, DN_H, P])
        dn_cst = small("dn_cst", [P, d["dn_consts"].shape[1]])
        after_eq, before = (dn_cst[:, i * P:(i + 1) * P] for i in range(2))
        level_mask = [dn_cst[:, (2 + i) * P:(3 + i) * P] for i in range(LEVELS + 1)]
        first_level, first_level_t = level_mask[LEVELS - 1], level_mask[LEVELS]
        ba = sb("ba", [P, 5, 8])
        rpb_raw = sb("rpb_raw", [P, 2, RPB_R - 1, GRID])
        dn_s = sb("dn_s", [P, 4, 5, DN_H])
        gate, beta = sb("gate", [P, 5, DN_H]), sb("beta", [P, 5, DN_H])
        dcol, edec, dlast, elast, bed, ea = (sb(n, [P, DN_H]) for n in ("dcol", "edec", "dlast", "elast", "bed", "ea"))
        w_ba = sb("w_ba", [P, DT, 8])
        w_ba_hi, w_ba_lo = sb("w_ba_hi", [P, DT, 8], f32r), sb("w_ba_lo", [P, DT, 8], f32r)
        ps = ctx.enter_context(nc.psum_tensor("ps", [P, 8 * BANK], f32))

        def bank(k):
            return ps[:, k * BANK:(k + 1) * BANK]

        def chunks(blk):
            return {0: [(0, 0, MEM)], 1: [(0, META, SEQ)], 2: [(0, 0, HALF), (BANK, HALF, HALF)]}[blk]

        def acc(s, blk):
            v = ps[:, s * 2 * BANK:(s + 1) * 2 * BANK]
            if blk == 2:
                return v.rearrange("p (c n) -> p c n", c=2)[:, :, 0:HALF]
            return v[:, 0:chunks(blk)[0][2]]

        def halves_of(t, blk):
            return t.rearrange("p (c n) -> p c n", c=2) if blk == 2 else t

        def span(blk):
            return slice(chunks(blk)[0][1], chunks(blk)[-1][1] + chunks(blk)[-1][2])

        def quad(k, n):
            return ps[:, k * BANK:k * BANK + DN_H * n].rearrange("p (h n) -> p h n", h=DN_H)

        def tn_segments(st):
            return {"l2": (qkv, [(0, 4, float(P) ** -0.5), (4, 4, 1.0)], 1.0),
                    "qk": (qk, [(0, 8, q_gain), (8, 2, k_gain)], 1.0 / HD),
                    "head": (qkv, [(8, 4, dn_gain)], 1.0 / P)}[st.what]

        mem_loaded, loaded = sem("mem_loaded"), sem("loaded")
        raw_full = [sem(f"raw_full{s}") for s in range(RING)]
        hi_done, lo_done, pe_done = sem("hi_done"), sem("lo_done"), sem("pe_done")
        acc_free = [sem(f"acc_free{s}") for s in range(RING)]
        x_done = sem("x_done")
        sq_ready, sq_added, ssq_done, ln_ready, rstd_ready = (
            sem(n) for n in ("sq_ready", "sq_added", "ssq_done", "ln_ready", "rstd_ready"))
        normed_ready, h_hi_ready, h_ready = (sem(n) for n in ("normed_ready", "h_hi_ready", "h_ready"))
        hi_staged, qk_staged, v_staged, s_done, s_read, max_ready, p_ready = (
            sem(n) for n in ("hi_staged", "qk_staged", "v_staged", "s_done", "s_read", "max_ready", "p_ready"))
        pt_done, pt_ready, pv_done, inv_ready, rec_ready = (
            sem(n) for n in ("pt_done", "pt_ready", "pv_done", "inv_ready", "rec_ready"))
        y_moved, y_ready, y_hi_ready, y_lo_ready = (sem(n) for n in ("y_moved", "y_ready", "y_hi_ready", "y_lo_ready"))
        alibi_full, rpb_full, rpb_masked = sem("alibi_full"), sem("rpb_full"), sem("rpb_masked")
        silu_ready, prod_ready, act_hi_ready, act_ready = (
            sem(n) for n in ("silu_ready", "prod_ready", "act_hi_ready", "act_ready"))
        padded_zero, gate_ready, tap_done, conv_ready = (
            sem(n) for n in ("padded_zero", "gate_ready", "tap_done", "conv_ready"))
        ev_in, ev_tap, ev_conv, ev_silu = (sem(n) for n in ("ev_in", "ev_tap", "ev_conv", "ev_silu"))
        ba_done, ba_dve, ba_act = sem("ba_done"), sem("ba_dve"), sem("ba_act")
        tn_sq, tn_ms, tn_rt, tn_r, tn_out = (sem(n) for n in ("tn_sq", "tn_ms", "tn_rt", "tn_r", "tn_out"))
        head_step, head_ready, head_hi, head_lo, gated_hi, gated_lo = (
            sem(n) for n in ("head_step", "head_ready", "head_hi", "head_lo", "gated_hi", "gated_lo"))
        d_pe, d_dve, d_act, d_pool = sem("d_pe"), sem("d_dve"), sem("d_act"), sem("d_pool")
        stored = sem("stored")

        N_FIRST, N_LOADS = 3, 6
        n_dn0, n_dn = delta_steps(META), delta_steps(P)

        def peeled(loop, n, body):
            body(0)
            if n > 1:
                with loop(1, n) as i:
                    body(i)

        def dn_at(which, c, name):
            if isinstance(c, int) and c == 0:
                return n_dn0[which].index(name) + 1
            return (c - 1) * len(n_dn[which]) + len(n_dn0[which]) + n_dn[which].index(name) + 1

        def dn_prev(which, c):
            if isinstance(c, int) and c <= 1:
                return c * len(n_dn0[which])
            return (c - 1) * len(n_dn[which]) + len(n_dn0[which])

        class Pair:

            def __init__(self, st, g, pos):
                self.st, self.g, self.pos = st, g, pos
                nb = len(st.blocks)
                self.b, self.slot, self.tile_slot = pos % nb, pos % 2, pos // nb
                self.c = st.blocks[self.b]
                self.nq, self.n = self.c["nq"], sum(n for _, n in self.c["keys"])
                self.tile = 2 * g + pos // nb
                self.count = g * (2 * nb) + (pos + st.pair0)
                self.exists = not isinstance(g, int) or g * 2 * nb + pos >= 0
                self.q = slice(self.c["q"], self.c["q"] + self.nq)

            def back(self, k):
                n = 2 * len(self.st.blocks)
                return Pair(self.st, self.g, self.pos - k) if self.pos >= k else Pair(self.st, self.g - 1, self.pos - k + n)

        def over_pairs(loop, st, body):
            def group(g):
                for pos in range(2 * len(st.blocks)):
                    body(Pair(st, g, pos))
            group(0)
            if st.nt > 2:
                with loop(1, st.nt // 2) as g:
                    group(g)

        def last_pair(st):
            return Pair(st, st.nt // 2 - 1, 2 * len(st.blocks) - 1)

        def counted(value):
            return not isinstance(value, int) or value >= 1

        block = ctx.enter_context(nc.Block())

        @block.sync
        def _(sp):
            sp.dma_start(mem_in[:, :, :], d["mem"].rearrange("(m p) t -> p m t", p=P)).then_inc(mem_loaded, 16)
            sp.dma_start(cst[:, :], d["consts"]).then_inc(mem_loaded, 16)
            sp.dma_start(vec[:, :], d["vectors"]).then_inc(mem_loaded, 16)
            for s in range(RING):
                sp.dma_start(raw[:, s, 0:UP * P], d["slabs8"][s]).then_inc(raw_full[s], 16)
            sp.dma_start(x[:, :, META:TOK], d["x"].rearrange("(m p) t -> p m t", p=P)).then_inc(loaded, 16)
            sp.dma_start(x[:, :, 0:META], d["meta"].rearrange("(m p) t -> p m t", p=P)).then_inc(loaded, 16)
            sp.dma_start(rows[:, 0:12], d["sink_a"].partition_broadcast(P)).then_inc(loaded, 16)
            sp.dma_start(rows[:, 12:28], d["sink_b"].partition_broadcast(P)).then_inc(loaded, 16)
            sp.dma_start(rows[:, 28:36], d["dn_rows"].partition_broadcast(P)).then_inc(loaded, 16)
            sp.dma_start(w_ba[:, :, :], d["w_ba"].rearrange("(m p) t -> p m t", p=P)).then_inc(loaded, 16)

            def load_slabs(q, s, size, src, at):
                sp.wait_ge(lo_done, 2 * q + s - 1)
                sp.dma_start(raw[:, s, 0:size * P], src[at]).then_inc(raw_full[s], 16)

            at, seen = RING, {UP: RING, DOWN: 0}

            def stream(upto):
                nonlocal at
                upto = min(upto, n_slabs)
                while at < upto:
                    size = kinds[at]
                    end = at
                    while end < upto and kinds[end] == size:
                        end += 2
                    src, first, q0 = d["slabs8" if size == UP else "slabs11"], seen[size], at // 2
                    with sp.Fori(0, (end - at) // 2) as i:
                        for s in range(RING):
                            load_slabs(i + q0, s, size, src, 2 * i + first + s)
                    seen[size] += end - at
                    at = end

            def load_bias(st, i):
                later = not isinstance(i, int)
                if st.bias == "alibi":
                    read, full = (i - 1) * len(st.blocks) + st.pair0, i * 16
                    dst, src = bias_sb[:, i % 2, :, 0:3 * P], d["alibi"][i]
                    if later or i >= 2:
                        sp.wait_ge(s_read, read)
                    if later or i >= 1:
                        sp.wait_ge(alibi_full, full)
                    sp.dma_start(dst, src).then_inc(alibi_full, 16)
                    return
                if later or i >= 1:
                    sp.wait_ge(rpb_masked, i * 2)
                for h in range(2):
                    for r in range(2):
                        src = d["rpb"]
                        off = (2 * i + h) * (RPB_R * RPB_W) + (1 - r) * RPB_W
                        sp.dma_start(rpb_raw[64 * r:64 * r + 64, h, :, :],
                                     bass.AP(src.tensor, off, [[1, GRID], [RPB_W, RPB_R - 1], [1, GRID]]))\
                            .then_inc(rpb_full, 16)

            for n, st in enumerate(stages):
                if st.kind == "even":
                    stream(st.slab0)
                    sp.wait_ge(y_lo_ready, st.pair0)
                    sp.dma_start(dn_cst[:, :], d["dn_consts"]).then_inc(loaded, 16)
                if st.kind == "proj":
                    nxt = next(t for t in stages[n:] if t.kind == "att")
                    if nxt.bias in ("alibi", "rpb"):
                        load_bias(nxt, 0)
                    stream(st.slab0 + st.nf + st.nv + 2)
                if st.kind == "att" and st.bias in ("alibi", "rpb"):
                    load_bias(st, 1)
                    for i in range(2, st.nt):
                        load_bias(st, i)
            stream(n_slabs)
            for s in range(RING):
                sp.wait_ge(acc_free[s], n_slabs // 2)
            sp.dma_start(d["out"].rearrange("(m p) t -> p m t", p=P), x[:, :, META:TOK]).then_inc(stored, 16)
            sp.wait_ge(stored, 16)

        @block.gpsimd
        def _(pool):
            def split_lo(q, s, size):
                pool.wait_ge(hi_done, 2 * q + s + 1)
                nc.gpsimd.tensor_tensor(w_lo[:, s, 0:size * P], raw[:, s, 0:size * P],
                                        w_hi[:, s, 0:size * P].bitcast(f32), ALU.subtract).then_inc(lo_done, 1)

            at = 0

            def stream(upto):
                nonlocal at
                upto = min(upto, n_slabs)
                while at < upto:
                    size, end = kinds[at], at
                    while end < upto and kinds[end] == size:
                        end += 2
                    q0 = at // 2
                    with pool.Fori(0, (end - at) // 2) as i:
                        for s in range(RING):
                            split_lo(i + q0, s, size)
                    at = end

            def prepare(st):
                nb = len(st.blocks)
                t = slice(0, TOK) if st.bias == "band" else slice(META, TOK)

                def split(hi, lo, src, done):
                    nc.gpsimd.tensor_copy(hi, src).then_inc(hi_staged, 1)
                    pool.wait_ge(hi_staged, done)
                    return nc.gpsimd.tensor_tensor(lo, src, hi.bitcast(f32), ALU.subtract)

                def read_before(i, sem_):
                    if not isinstance(i, int) or (i - 1) * nb + st.pair0 >= 1:
                        pool.wait_ge(sem_, (i - 1) * nb + st.pair0)

                def stage_q(i):
                    read_before(i, s_done)
                    split(q_hi[:, i % 2, t], q_lo[:, i % 2, t], qk[:, st.qt + i, t], 2 * (i + st.tile0) + 1)

                def stage_k(i):
                    if st.bias == "band":
                        at = i // st.group + st.kt
                        keys = qk[:, at, META:TOK].rearrange("p (b n) -> p b n", n=P)
                        meta = qk[:, at, 0:META].unsqueeze(1).to_broadcast([P, 4, META])
                        hi, lo = (k[:, i % 2, :].rearrange("p (b n) -> p b n", n=KEY_STEP) for k in (k_hi, k_lo))
                        nc.gpsimd.tensor_copy(hi[:, :, P:KEY_STEP], meta)
                        nc.gpsimd.tensor_copy(hi[:, :, 0:P], keys).then_inc(hi_staged, 1)
                        pool.wait_ge(hi_staged, 2 * (i + st.tile0) + 2)
                        nc.gpsimd.tensor_tensor(lo[:, :, P:KEY_STEP], meta, hi[:, :, P:KEY_STEP].bitcast(f32),
                                                ALU.subtract)
                        nc.gpsimd.tensor_tensor(lo[:, :, 0:P], keys, hi[:, :, 0:P].bitcast(f32),
                                                ALU.subtract).then_inc(qk_staged, 1)
                        return
                    if st.bias is None:
                        src, kt = mk[:, st.layer, i, :], slice(0, MEM)
                    else:
                        src, kt = qk[:, i // st.group + st.kt, t], t
                    split(k_hi[:, i % 2, kt], k_lo[:, i % 2, kt], src, 2 * (i + st.tile0) + 2).then_inc(qk_staged, 1)

                def stage_v(i):
                    read_before(i, pv_done)
                    if st.bias is None:
                        src = mv[:, st.layer, :, bass.ds(i * P, P)]
                    else:
                        src = val[:, 0:4, bass.ds((i // st.group) * P, P)]
                    n = 2 if st.bias is None else 4
                    last = nc.gpsimd.tensor_copy(v_st[:, i % 2, 0:n, :], src)
                    if st.bias == "band":
                        last = nc.gpsimd.tensor_copy(v_st[0:META, i % 2, 4, :],
                                                     val[0:META, 4, bass.ds((i // st.group) * P, P)])
                    last.then_inc(v_staged, 1)

                def mask(i):
                    if st.bias != "rpb":
                        return
                    pool.wait_ge(rpb_full, i * 64 + 64)
                    read_before(i, s_read)
                    for h in range(2):
                        nc.gpsimd.tensor_tensor(
                            bias_sb[:, i % 2, h, :].rearrange("p (r c) -> p r c", c=GRID), rpb_raw[:, h, :, ::-1],
                            grid_mask.unsqueeze(1).to_broadcast([P, RPB_R - 1, GRID]), ALU.add)\
                            .then_inc(rpb_masked, 1)

                return [stage_q, stage_k, stage_v, mask]

            def attend(st, nxt, nv):
                nb = len(st.blocks)

                def y_lo(i, b):
                    c = st.blocks[b]
                    q = slice(c["q"], c["q"] + c["nq"])
                    k = i * nb + (b + st.pair0)
                    pool.wait_ge(y_hi_ready, k + 1)
                    nc.gpsimd.tensor_tensor(h_lo[:, st.y + i, q], y_sb[:, (i * nb + b) % 2, 0:c["nq"]],
                                            h_hi[:, st.y + i, q].bitcast(f32), ALU.subtract).then_inc(y_lo_ready, 1)
                chores = prepare(st)
                if nv:
                    for s in range(RING):
                        pool.wait_ge(acc_free[s], (st.slab0 - nv) // 2)
                    if st.bias == "band":
                        pool.wait_ge(tn_out, st.tn0)
                    chores[0](0)
                    chores[1](0)
                    chores[3](0)
                    for s in range(RING):
                        pool.wait_ge(acc_free[s], st.slab0 // 2)
                    chores[2](0)
                    stream(st.slab0 + 2)

                def tile(i, chores, tile0):
                    for b in range(nb):
                        if b < 4 and chores:
                            chores[b](tile0)
                        if b >= 3:
                            y_lo(i - 1, b - 3)
                        elif not isinstance(i, int) or i >= 2:
                            y_lo(i - 2, b - 3 + nb)
                tile(1, chores, 1)
                if st.nt > 2:
                    with pool.Fori(2, st.nt) as i:
                        tile(i, chores, i)
                tile(st.nt, prepare(nxt) if nxt else None, 0)
                for b in range(nb - 3, nb):
                    y_lo(st.nt - 1, b)

            def norm_lo(st):
                stream(st.slab0 + 2)
                t = span(st.blk)
                for k in range(DT):
                    pool.wait_ge(h_hi_ready, DT * st.nh0 + k + 1)
                    nc.gpsimd.tensor_tensor(h_lo[:, k, t], normed[:, k % 2, t], h_hi[:, k, t].bitcast(f32),
                                            ALU.subtract).then_inc(h_ready, 1)

            def gated_split(st):
                pool.wait_ge(ba_done, 1)
                for s in range(RING):
                    pool.wait_ge(acc_free[s], st.slab0 // 2)
                for m in range(4):
                    nc.gpsimd.tensor_copy(h_hi[:, m, :], conv_y[:, m, :]).then_inc(gated_hi, 1)
                    pool.wait_ge(gated_hi, m + 1)
                    nc.gpsimd.tensor_tensor(h_lo[:, m, :], conv_y[:, m, :], h_hi[:, m, :].bitcast(f32),
                                            ALU.subtract).then_inc(gated_lo, 1)

            def head_split():
                for j in range(4):
                    pool.wait_ge(head_hi, j + 1)
                    nc.gpsimd.tensor_tensor(h_lo[:, 4 + j, :], normed_o[:, j % 2, :],
                                            h_hi[:, 4 + j, :].bitcast(f32), ALU.subtract).then_inc(head_lo, 1)

            def delta():
                def chunk(c, n):
                    levels = delta_steps(n)[0]
                    pool.wait_ge(loaded, 16 * N_LOADS + 16)
                    pool.wait_ge(d_dve, dn_at(2, c, "at"))
                    for s in levels:
                        if s - 2 in levels:
                            pool.wait_ge(d_pe, dn_at(1, c, ("z", s - 2)))
                        nc.gpsimd.tensor_tensor(a_lv[0:n, s % 2, :, 0:n], a_t[0:n, :, 0:n],
                                                level_mask[s - 1][0:n, 0:n].unsqueeze(1).to_broadcast([n, DN_H, n]),
                                                ALU.mult).then_inc(d_pool, 1)
                chunk(0, META)
                with pool.Fori(1, 5) as c:
                    chunk(c, P)

            for n, st in enumerate(stages):
                if st.kind == "norm" and st.src != "final":
                    norm_lo(st)
                if st.kind == "tn" and st.what == "l2":
                    stream(st.slab0)
                    gated_split(st)
                    stream(st.slab0 + 2)
                if st.kind == "delta":
                    delta()
                if st.kind == "tn" and st.what == "head":
                    head_split()
                if st.kind == "proj":
                    stream(st.slab0 + st.nf + st.nv)
                if st.kind == "att":
                    nxt = stages[n + 1] if stages[n + 1].kind == "att" else None
                    before = next(t for t in reversed(stages[:n]) if t.kind in ("proj", "att"))
                    attend(st, nxt, before.nv)
            stream(n_slabs)

        @block.scalar
        def _(act):
            def split_hi(q, s, size=UP):
                if isinstance(q, int) and 2 * q + s >= n_slabs:
                    return
                act.wait_ge(raw_full[s], 16 * q + 16)
                if not (isinstance(q, int) and q == 0):
                    act.wait_ge(pe_done, 2 * q + s - 1)
                nc.scalar.activation(w_hi[:, s, 0:size * P], raw[:, s, 0:size * P], ACT.Copy).then_inc(hi_done, 1)

            def square(st, k, s):
                n = DT * st.norm0 + k
                if counted(n - 1):
                    act.wait_ge(sq_added, n - 1)
                src, t = mem_in if st.src == "mem" else x, span(st.blk)
                nc.scalar.activation(sq[:, s, t], src[:, k, t], ACT.Square).then_inc(sq_ready, 1)

            def split_ahead(q0, n, size=UP, squares=None):
                with act.Fori(0, n) as i:
                    for s in range(RING):
                        split_hi(i + (q0 + 1), s, size)
                        if squares:
                            act.wait_ge(acc_free[s], i + (q0 + 1))
                            square(squares, 2 * i + s, s)

            def norm(st):
                t = span(st.blk)
                if st.after == "loads" and st.src != "mem":
                    act.wait_ge(loaded, 16 * N_LOADS)
                if st.after != "slabs":
                    for k in range(DT):
                        if st.after == "final":
                            act.wait_ge(x_done, k + 1)
                        square(st, k, k % 2)
                if st.src == "mem":
                    for s in range(RING):
                        split_hi(0, s)
                act.wait_ge(ssq_done, st.norm0 + 1)
                nc.scalar.activation(halves_of(rstd[:, t], st.blk), acc(2, st.blk), ACT.Ln, scale=1.0 / D,
                                     bias=eps_col).then_inc(ln_ready, 1)
                act.wait_ge(ln_ready, st.norm0 + 1)
                nc.scalar.activation(rstd[:, t], rstd[:, t], ACT.Exp, scale=-0.5).then_inc(rstd_ready, 1)
                if st.src == "final":
                    return
                for k in range(DT):
                    act.wait_ge(normed_ready, DT * st.nh0 + k + 1)
                    nc.scalar.activation(h_hi[:, k, t], normed[:, k % 2, t], ACT.Copy).then_inc(h_hi_ready, 1)

            def attend(st):
                off = 1 if st.sink is None else 0

                def probs(p, h):
                    act.wait_ge(max_ready, p.count + 1)
                    s_h = s_sb[0:p.nq, p.slot, h, off:p.n + 1]
                    nc.scalar.activation(s_h, s_h, ACT.Exp, bias=n_max[0:p.nq, p.slot, h:h + 1], scale=1.0,
                                         accum_out=p_sum[0:p.nq, p.slot, h:h + 1]).then_inc(p_ready, 1)

                def turned(p, h):
                    cs = p.c["chunks"]
                    full = sum(1 for ch in cs if ch[1] == P)
                    act.wait_ge(pt_done, 2 * p.count + h + 1)
                    if counted(p.count):
                        act.wait_ge(pv_done, p.count)
                    src = bank(4 + h).rearrange("p (c n) -> p c n", n=P)
                    last = None
                    if full:
                        last = nc.scalar.activation(p_t[:, h, 0:full, 0:p.nq], src[:, 0:full, 0:p.nq], ACT.Copy)
                    if full < len(cs):
                        last = nc.scalar.activation(p_t[0:META, h, full, 0:p.nq], src[0:META, full, 0:p.nq],
                                                    ACT.Copy)
                    last.then_inc(pt_ready, 1)

                def spread(p):
                    act.wait_ge(inv_ready, p.count + 1)
                    if counted(p.count - 1):
                        act.wait_ge(pv_done, p.count - 1)
                    nc.scalar.activation(p_rec[0:p.nq, p.slot, :].rearrange("p (h n) -> p h n", h=2),
                                         p_inv[0:p.nq, p.slot, :].unsqueeze(2).to_broadcast([p.nq, 2, HD]),
                                         ACT.Copy).then_inc(rec_ready, 1)

                def move_y(p):
                    act.wait_ge(pv_done, p.count + 1)
                    if counted(p.count - 1):
                        act.wait_ge(y_lo_ready, p.count - 1)
                    nc.scalar.activation(y_sb[:, p.slot, 0:p.nq], bank(6 + p.slot)[:, 0:p.nq], ACT.Copy)\
                        .then_inc(y_moved, 1)

                def y_hi(p):
                    act.wait_ge(y_ready, p.count + 1)
                    nc.scalar.activation(h_hi[:, st.y + p.tile, p.q], y_sb[:, p.slot, 0:p.nq],
                                         ACT.Copy).then_inc(y_hi_ready, 1)

                def step(p):
                    if p.back(2).exists:
                        move_y(p.back(2))
                    if p.back(3).exists:
                        y_hi(p.back(3))
                    for h in range(2):
                        if p.back(1).exists:
                            turned(p.back(1), h)
                        probs(p, h)
                    if p.back(1).exists:
                        spread(p.back(1))
                over_pairs(act.Fori, st, step)
                last = last_pair(st)
                move_y(last.back(1))
                y_hi(last.back(2))
                for h in range(2):
                    turned(last, h)
                spread(last)
                move_y(last)
                y_hi(last.back(1))
                y_hi(last)

            def ffn(st):
                g0 = st.ffn0 * FF_T
                for g in range(FF_G):
                    q0 = (st.slab0 + g * (2 * FF_J + DT)) // 2

                    def body(j, ahead):
                        done = j + g0 + g * FF_J
                        split_hi(j + q0 + 1, 0, ahead)
                        if st.conv:
                            c0 = done - 2 * FF_T
                            act.wait_ge(pe_done, 2 * (j + q0) + 1)
                            act.wait_ge(padded_zero, st.ffn0 + 1)
                            nc.scalar.activation(halves_of(padded[:, 0, 3:3 + TOK], 2), acc(0, 2), ACT.Copy)\
                                .then_inc(acc_free[0], 1)
                            act.wait_ge(conv_ready, c0 + 1)
                            act.wait_ge(prod_ready, done)
                            nc.scalar.activation(silu_g[:, :], conv[:, 0, :], ACT.Silu).then_inc(silu_ready, 1)
                        else:
                            act.wait_ge(pe_done, 2 * (j + q0) + 1)
                            if not isinstance(done, int) or done >= 1:
                                act.wait_ge(prod_ready, done)
                            nc.scalar.activation(silu_g[:, span(st.blk)], acc(0, st.blk), ACT.Silu)\
                                .then_inc(acc_free[0], 1)
                        split_hi(j + q0 + 1, 1, ahead)
                    body(0, UP)
                    with act.Fori(1, FF_J - 1) as j:
                        body(j, UP)
                    body(FF_J - 1, DOWN)
                    squares = st.next_norm if g == FF_G - 1 else None
                    split_ahead(q0 + FF_J, DT // 2 - 1, DOWN, squares)
                    for s in range(RING):
                        split_hi(q0 + FF_J + DT // 2, s)
                        if squares:
                            act.wait_ge(acc_free[s], q0 + FF_J + DT // 2)
                            square(squares, DT - RING + s, s)

            def even(st):
                q0 = st.slab0 // 2
                split_ahead(q0, 6)
                with act.Fori(0, 6) as i:
                    for s in range(RING):
                        split_hi(i + (q0 + 7), s)
                    for s in range(RING):
                        act.wait_ge(ev_conv, 2 * i + s + 1)
                        nc.scalar.activation(qkv[:, 2 * i + s, :], conv[:, s, :], ACT.Silu).then_inc(ev_silu, 1)
                with act.Fori(0, 2) as i:
                    for s in range(RING):
                        split_hi(i + (q0 + 13), s)
                    for s in range(RING):
                        act.wait_ge(pe_done, 2 * (i + q0 + 12) + s + 1)
                        nc.scalar.activation(halves_of(zed[:, 2 * i + s, :], 2), acc(s, 2), ACT.Silu)\
                            .then_inc(acc_free[s], 1)
                act.wait_ge(ba_dve, 4)
                nc.scalar.activation(dn_s[:, 1, :, :], ba[:, :, 0:DN_H], ACT.Exp, scale=-1.0).then_inc(ba_act, 1)
                nc.scalar.activation(dn_s[:, 3, :, :], dn_s[:, 2, :, :], ACT.Exp).then_inc(ba_act, 1)
                nc.scalar.activation(ea[:, :], a_log, ACT.Exp).then_inc(ba_act, 1)
                act.wait_ge(ba_act, 2)
                nc.scalar.activation(dn_s[:, 3, :, :], dn_s[:, 3, :, :], ACT.Ln, bias=1.0).then_inc(ba_act, 1)

            def tile_norm(st):
                buf, segs, scale = tn_segments(st)
                done = st.tn0
                for start, n, _ in segs:
                    def body(i):
                        for s in range(RING):
                            nc.scalar.activation(sq[:, s, :], buf[:, 2 * i + s + start, :], ACT.Square)\
                                .then_inc(tn_sq, 1)
                        for s in range(RING):
                            j = 2 * i + s + done
                            act.wait_ge(tn_ms, j + 1)
                            if not isinstance(j, int) or j >= 2:
                                act.wait_ge(tn_out, j - 1)
                            nc.scalar.activation(halves_of(root[:, s, :], 2), acc(2 + s, 2), ACT.Ln, scale=scale,
                                                 bias=eps_col).then_inc(tn_rt, 1)
                        for s in range(RING):
                            act.wait_ge(tn_rt, 2 * i + s + done + 1)
                            nc.scalar.activation(root[:, s, :], root[:, s, :], ACT.Exp, scale=-0.5).then_inc(tn_r, 1)
                        if st.what == "head":
                            for s in range(RING):
                                act.wait_ge(head_ready, 2 * i + s + 1)
                                nc.scalar.activation(h_hi[:, 4 + 2 * i + s, :], normed_o[:, s, :], ACT.Copy)\
                                    .then_inc(head_hi, 1)
                    if st.what == "l2":
                        act.wait_ge(ev_silu, 12)
                    if st.what == "qk":
                        for s in range(RING):
                            act.wait_ge(acc_free[s], st.slab0 // 2)
                    if st.what == "head":
                        act.wait_ge(d_dve, dn_prev(2, 5))
                    peeled(act.Fori, n // 2, body)
                    done += n

            def delta():
                def chunk(c, n):
                    levels = delta_steps(n)[0]

                    def need(which, name):
                        act.wait_ge((None, d_pe, d_dve, d_act, d_pool)[which], dn_at(which, c, name))
                    need(2, "dlast")
                    nc.scalar.activation(erow[:, :, 0:n], row[:, :, 0:n], ACT.Exp).then_inc(d_act, 1)
                    nc.scalar.activation(edec[0:n, :], dcol[0:n, :], ACT.Exp).then_inc(d_act, 1)
                    nc.scalar.activation(elast[0:n, :], dlast[0:n, :], ACT.Exp).then_inc(d_act, 1)
                    need(2, "dtm")
                    nc.scalar.activation(dt_[0:n, :, 0:n], dt_[0:n, :, 0:n], ACT.Exp).then_inc(d_act, 1)
                    need(2, "dlm")
                    nc.scalar.activation(dl_[0:n, :, 0:n], dl_[0:n, :, 0:n], ACT.Exp).then_inc(d_act, 1)
                    for s in levels:
                        need(1, ("z", s))
                        nc.scalar.activation(z_m[0:n, :, 0:n], quad(4, n)[0:n], ACT.Copy).then_inc(d_act, 1)
                    need(1, "vn")
                    nc.scalar.activation(v_new[0:n, :, :], quad(5, P)[0:n], ACT.Copy).then_inc(d_act, 1)
                chunk(0, META)
                with act.Fori(1, 5) as c:
                    chunk(c, P)

            act.wait_ge(mem_loaded, 16 * N_FIRST)
            for st in stages:
                if st.kind == "norm":
                    norm(st)
                elif st.kind == "memkv":
                    split_ahead(st.slab0 // 2, 4)
                elif st.kind == "proj":
                    split_ahead(st.slab0 // 2, (st.nf + st.nv) // 2)
                elif st.kind == "out":
                    split_ahead(st.slab0 // 2, DT // 2, squares=st.next_norm)
                elif st.kind == "att":
                    attend(st)
                elif st.kind == "ffn":
                    ffn(st)
                elif st.kind == "even":
                    even(st)
                elif st.kind == "tn":
                    tile_norm(st)
                elif st.kind == "delta":
                    delta()

        @block.tensor
        def _(pe):
            def begin(q, s):
                pe.wait_ge(lo_done, 2 * q + s + 1)
                if not isinstance(q, int) or q >= 1:
                    pe.wait_ge(acc_free[s], q)

            def slab(q, s, blk, nb=UP, hi=h_hi, lo=h_lo):
                begin(q, s)
                for k in range(nb):
                    wk = slice(k * P, (k + 1) * P)
                    for w, a in ((w_hi, hi), (w_hi, lo), (w_lo, hi)):
                        for po, to, n in chunks(blk):
                            last = nc.tensor.matmul(
                                ps[:, s * 2 * BANK + po:s * 2 * BANK + po + n], w[:, s, wk], a[:, k, to:to + n],
                                start=(k == 0 and w is w_hi and a is hi), stop=(k == nb - 1 and w is w_lo))
                last.then_inc(pe_done, 1)

            def slab_tokens(q, s, toks):
                begin(q, s)
                for j, (t0, n) in enumerate(toks):
                    out = ps[0:n, s * 2 * BANK + j * P:s * 2 * BANK + (j + 1) * P]
                    for k in range(DT):
                        wk = slice(k * P, (k + 1) * P)
                        for w, a in ((w_hi, h_hi), (w_hi, h_lo), (w_lo, h_hi)):
                            last = nc.tensor.matmul(out, a[:, k, t0:t0 + n], w[:, s, wk],
                                                    start=(k == 0 and w is w_hi and a is h_hi),
                                                    stop=(k == DT - 1 and w is w_lo))
                last.then_inc(pe_done, 1)

            def first_slabs(q, blk, nh0):
                for s in range(RING):
                    begin(q, s)
                for k in range(DT):
                    pe.wait_ge(h_ready, DT * (nh0 - 1) + k + 1)
                    wk = slice(k * P, (k + 1) * P)
                    for s in range(RING):
                        for w, a in ((w_hi, h_hi), (w_hi, h_lo), (w_lo, h_hi)):
                            for po, to, n in chunks(blk):
                                last = nc.tensor.matmul(
                                    ps[:, s * 2 * BANK + po:s * 2 * BANK + po + n], w[:, s, wk], a[:, k, to:to + n],
                                    start=(k == 0 and w is w_hi and a is h_hi), stop=(k == DT - 1 and w is w_lo))
                        if k == DT - 1:
                            last.then_inc(pe_done, 1)

            def many(q0, n, blk, **kw):
                with pe.Fori(0, n) as i:
                    for s in range(RING):
                        slab(i + q0, s, blk, **kw)

            def norm(st):
                pe.wait_ge(sq_added, DT * (st.norm0 + 1))
                if st.norm0:
                    pe.wait_ge(ln_ready, st.norm0)
                for po, to, n in chunks(st.blk):
                    last = nc.tensor.matmul(ps[:, 4 * BANK + po:4 * BANK + po + n], ones, sq_sum[:, to:to + n],
                                            start=True, stop=True)
                last.then_inc(ssq_done, 1)

            def memkv(st):
                for layer in range(2):
                    q = st.slab0 // 2 + 2 * layer
                    if layer == 0:
                        first_slabs(q, 0, st.nh0)
                    for s in range(RING * (layer == 1)):
                        slab(q, s, 0)
                    for s in range(RING):
                        slab_tokens(q + 1, s, [(0, P), (P, P)])

            def proj(st):
                first_slabs(st.slab0 // 2, st.blk, st.nh0)
                many(st.slab0 // 2 + 1, st.nf // 2 - 1, st.blk)
                toks = [(META + P * b, P) for b in range(4)] + [(0, META)] * (st.blk == 2)
                q0 = (st.slab0 + st.nf) // 2
                if st.nv == 2:
                    for s in range(RING):
                        slab_tokens(q0, s, toks)
                else:
                    with pe.Fori(0, st.nv // 2) as i:
                        for s in range(RING):
                            slab_tokens(i + q0, s, toks)

            def attend(st):
                def scores(p):
                    if p.b == 0:
                        pe.wait_ge(qk_staged, p.tile + (st.tile0 + 1))
                    if counted(p.count - 1):
                        pe.wait_ge(s_read, p.count - 1)
                    col = 0
                    for k0, n in p.c["keys"]:
                        for a, b in ((q_hi, k_hi), (q_hi, k_lo), (q_lo, k_hi)):
                            for h in range(2):
                                hp = slice(HD * h, HD * h + HD)
                                last = nc.tensor.matmul(bank(2 * p.slot + h)[0:p.nq, col:col + n],
                                                        a[hp, p.tile_slot, p.q], b[hp, p.tile_slot, k0:k0 + n],
                                                        start=(b is k_hi and a is q_hi), stop=(a is q_lo))
                        col += n
                    last.then_inc(s_done, 1)

                def turn(p):
                    for h in range(2):
                        u = 2 * p.count + h
                        pe.wait_ge(p_ready, u + 1)
                        if counted(u - 1):
                            pe.wait_ge(pt_ready, u - 1)
                        for j, (col, n, _) in enumerate(p.c["chunks"]):
                            last = nc.tensor.transpose(bank(4 + h)[0:n, j * P:j * P + p.nq],
                                                       s_sb[0:p.nq, p.slot, h, 1 + col:1 + col + n],
                                                       ident[0:p.nq, 0:p.nq])
                        last.then_inc(pt_done, 1)

                def values(p):
                    out = bank(6 + p.slot)
                    if p.b == 0:
                        pe.wait_ge(v_staged, p.tile + (st.tile0 + 1))
                    if counted(p.count - 1):
                        pe.wait_ge(y_ready, p.count - 1)
                    for h in range(2):
                        pe.wait_ge(pt_ready, 2 * p.count + h + 1)
                        cs = p.c["chunks"]
                        for j, (_, n, vb) in enumerate(cs):
                            nc.tensor.matmul(out[HD * h:HD * h + HD, 0:p.nq],
                                             v_st[0:n, p.tile_slot, vb, HD * h:HD * h + HD],
                                             p_t[0:n, h, j, 0:p.nq], start=(j == 0), stop=(j == len(cs) - 1))
                    pe.wait_ge(rec_ready, p.count + 1)
                    nc.tensor.transpose(out[:, P:P + p.nq],
                                        p_rec[0:p.nq, p.slot, :],
                                        ident[0:p.nq, 0:p.nq]).then_inc(pv_done, 1)

                def step(p):
                    scores(p)
                    if p.back(2).exists:
                        values(p.back(2))
                    if p.back(1).exists:
                        turn(p.back(1))
                for s in range(RING):
                    pe.wait_ge(acc_free[s], st.slab0 // 2)
                if st.bias == "band":
                    for g in range(st.nt // 2):
                        for pos in range(2 * len(st.blocks)):
                            step(Pair(st, g, pos))
                else:
                    over_pairs(pe.Fori, st, step)
                last = last_pair(st)
                values(last.back(1))
                turn(last)
                values(last)

            def ffn(st):
                for g in range(FF_G):
                    q0 = (st.slab0 + g * (2 * FF_J + DT)) // 2
                    if g == 0:
                        first_slabs(q0, st.blk, st.nh0)
                    many(q0 + (g == 0), FF_J - (g == 0), st.blk)
                    pe.wait_ge(act_ready, st.ffn0 * FF_T + (g + 1) * FF_J)
                    many(q0 + FF_J, DT // 2, st.blk, nb=DOWN, hi=act_hi, lo=act_lo)

            def even(st):
                first_slabs(st.slab0 // 2, 2, st.nh0)
                many(st.slab0 // 2 + 1, 13, 2)
                pe.wait_ge(ba_dve, 2)
                for c in range(5):
                    n, t0 = (META, 0) if c == 0 else (P, META + P * (c - 1))
                    for k in range(DT):
                        for w, a in ((w_ba_hi, h_hi), (w_ba_hi, h_lo), (w_ba_lo, h_hi)):
                            last = nc.tensor.matmul(bank(4)[0:n, 8 * c:8 * c + 8], a[:, k, t0:t0 + n], w[:, k, :],
                                                    start=(k == 0 and w is w_ba_hi and a is h_hi),
                                                    stop=(k == DT - 1 and w is w_ba_lo))
                last.then_inc(ba_done, 1)

            def tile_norm(st):
                buf, segs, _ = tn_segments(st)
                done = st.tn0
                matrix = halves if st.what == "qk" else ones
                if st.what == "l2":
                    pe.wait_ge(ba_dve, 4)
                for _, n, _ in segs:
                    with pe.Fori(0, n // 2) as i:
                        for s in range(RING):
                            pe.wait_ge(tn_sq, 2 * i + s + done + 1)
                            for po, to, m in chunks(2):
                                last = nc.tensor.matmul(ps[:, (4 + 2 * s) * BANK + po:(4 + 2 * s) * BANK + po + m],
                                                        matrix, sq[:, s, to:to + m], start=True, stop=True)
                            last.then_inc(tn_ms, 1)
                    done += n

            def delta():
                def chunk(c, n):
                    levels = delta_steps(n)[0]
                    t0 = 0 if isinstance(c, int) else P * c + (META - P)

                    def need(which, name):
                        pe.wait_ge((None, d_pe, d_dve, d_act, d_pool)[which], dn_at(which, c, name))

                    def heads(out, lhs, rhs, inc=True, start=True, stop=True):
                        for h in range(DN_H):
                            last = nc.tensor.matmul(out[:, h, :], lhs(h), rhs(h), start=start, stop=stop)
                        if inc:
                            last.then_inc(d_pe, 1)
                    need(2, "gb")
                    heads(quad(0, n), lambda h: gb[0:n, h, :], lambda h: tri[0:n, 0:n], inc=False)
                    nc.tensor.matmul(bank(1)[0:n, 0:DN_H], tri[0:n, 0:n], gate[0:n, c, :], start=True, stop=True)\
                        .then_inc(d_pe, 1)
                    heads(quad(2, n)[0:n], lambda h: kc[:, h, 0:n], lambda h: kc[:, h, 0:n])
                    heads(quad(3, n)[0:n], lambda h: kc[:, h, 0:n], lambda h: qkv[:, h, bass.ds(t0, n)])
                    need(2, "a")
                    for h in range(DN_H):
                        last = nc.tensor.transpose(quad(1, n)[0:n, h, :], a_m[0:n, h, 0:n], ident[0:n, 0:n])
                    last.then_inc(d_pe, 1)
                    for s in levels:
                        first = s == levels[0]
                        need(4, ("am", s))
                        need(2, "x" if first else ("x", s - 1))
                        heads(quad(4, n)[0:n], lambda h: a_lv[0:n, s % 2, h, 0:n], lambda h: x_m[0:n, h, 0:n])
                        need(3, ("z", s))
                        need(2, "xt" if first else ("xt", s - 1))
                        if s != levels[-1]:
                            heads(quad(5, n)[0:n], lambda h: x_t[0:n, h, 0:n], lambda h: z_m[0:n, h, 0:n])
                        heads(quad(6, n)[0:n], lambda h: z_m[0:n, h, 0:n], lambda h: x_t[0:n, h, 0:n])
                    for h in range(DN_H):
                        last = nc.tensor.transpose(quad(7, P)[0:n, h, :], vc[:, h, 0:n], ident)
                    last.then_inc(d_pe, 1)
                    heads(quad(3, P)[0:n], lambda h: kc[:, h, 0:n], lambda h: state[:, h, :])
                    for h in range(DN_H):
                        last = nc.tensor.transpose(quad(2, P)[0:n, h, :], kc[:, h, 0:n], ident)
                    last.then_inc(d_pe, 1)
                    need(2, "r")
                    heads(quad(5, P)[0:n], lambda h: x_t[0:n, h, 0:n], lambda h: res[0:n, h, :])
                    need(2, "qd")
                    need(3, "vn")
                    for h in range(DN_H):
                        nc.tensor.matmul(quad(6, n)[:, h, :], state[:, h, :], q_dec[:, h, 0:n], start=True, stop=False)
                        last = nc.tensor.matmul(quad(6, n)[:, h, :], v_new[0:n, h, :], qk_t[0:n, h, 0:n],
                                                start=False, stop=True)
                    last.then_inc(d_pe, 1)
                    heads(quad(4, P), lambda h: k_dec[0:n, h, :], lambda h: v_new[0:n, h, :])
                chunk(0, META)
                with pe.Fori(1, 5) as c:
                    chunk(c, P)

            pe.wait_ge(mem_loaded, 16 * N_FIRST)
            for st in stages:
                if st.kind == "norm":
                    norm(st)
                elif st.kind == "memkv":
                    memkv(st)
                elif st.kind == "proj":
                    proj(st)
                elif st.kind == "att":
                    attend(st)
                elif st.kind == "out":
                    if st.y2:
                        pe.wait_ge(gated_lo, 4)
                        pe.wait_ge(head_lo, 4)
                    else:
                        pe.wait_ge(y_lo_ready, st.pair0)
                    many(st.slab0 // 2, DT // 2, st.blk)
                elif st.kind == "ffn":
                    ffn(st)
                elif st.kind == "even":
                    even(st)
                elif st.kind == "tn":
                    tile_norm(st)
                elif st.kind == "delta":
                    delta()

        @block.vector
        def _(dve):
            busy = [False]

            def settle():
                if busy[0]:
                    dve.drain()
                busy[0] = False

            @contextmanager
            def loop(first, end):
                settle()
                with dve.Fori(first, end) as i:
                    yield i
                    settle()

            def wait(sem_, value):
                settle()
                dve.wait_ge(sem_, value)

            def stt(*a, **kw):
                settle()
                busy[0] = True
                return nc.vector.scalar_tensor_tensor(*a, **kw)

            def tt(*a, **kw):
                settle()
                busy[0] = True
                return nc.vector.tensor_tensor(*a, **kw)

            def ts(*a, **kw):
                settle()
                busy[0] = True
                return nc.vector.tensor_scalar(*a, **kw)

            def copy(*a, **kw):
                settle()
                busy[0] = True
                return nc.vector.tensor_copy(*a, **kw)

            def recip(*a, **kw):
                settle()
                busy[0] = True
                return nc.vector.reciprocal(*a, **kw)

            def reduce(*a, **kw):
                settle()
                busy[0] = True
                return nc.vector.tensor_reduce(*a, **kw)

            def fill(*a, **kw):
                settle()
                busy[0] = True
                return nc.vector.memset(*a, **kw)

            def ended(q, s):
                wait(pe_done, 2 * q + s + 1)

            def clear_sum(st):
                if st.norm0:
                    wait(ssq_done, st.norm0)
                fill(sq_sum[:, span(st.blk)], 0.0)

            def add_square(st, k, s):
                t = span(st.blk)
                wait(sq_ready, DT * st.norm0 + k + 1)
                tt(sq_sum[:, t], sq_sum[:, t], sq[:, s, t], ALU.add).then_inc(sq_added, 1)

            def norm(st):
                src = mem_in if st.src == "mem" else x
                t = span(st.blk)
                if st.after != "slabs":
                    clear_sum(st)
                    for k in range(DT):
                        add_square(st, k, k % 2)
                wait(rstd_ready, st.norm0 + 1)
                for k in range(DT):
                    g = gains[:, st.gain, k:k + 1]
                    if st.src == "final":
                        stt(x[:, k, t], x[:, k, t], g, rstd[:, t], ALU.mult, ALU.mult)\
                            .then_inc(x_done, 1)
                        continue
                    if k >= 2:
                        wait(h_ready, DT * st.nh0 + k - 1)
                    stt(normed[:, k % 2, t], src[:, k, t], g, rstd[:, t], ALU.mult, ALU.mult)\
                        .then_inc(normed_ready, 1)

            def memkv(st):
                for layer in range(2):
                    q = st.slab0 // 2 + 2 * layer
                    for s in range(RING):
                        ended(q, s)
                        copy(mk[:, layer, s, :], acc(s, 0)).then_inc(acc_free[s], 1)
                    for s in range(RING):
                        ended(q + 1, s)
                        copy(mv[:, layer, :, s * P:(s + 1) * P],
                                              acc(s, 0).rearrange("p (b n) -> p b n", b=2)).then_inc(acc_free[s], 1)

            def proj(st):
                q0 = st.slab0 // 2
                with loop(0, st.nf // 2) as i:
                    for s in range(RING):
                        ended(i + q0, s)
                        copy(halves_of(qk[:, 2 * i + s, span(st.blk)], st.blk), acc(s, st.blk))\
                            .then_inc(acc_free[s], 1)
                q1 = q0 + st.nf // 2

                def v_tile(i, s):
                    ended(i + q1, s)
                    last = copy(
                        val[:, 0:4, bass.ds((2 * i + s) * P, P)],
                        bank(2 * s).rearrange("p (b n) -> p b n", b=4))
                    if st.blk == 2:
                        last = copy(val[0:META, 4, bass.ds((2 * i + s) * P, P)],
                                                     bank(2 * s + 1)[0:META, 0:P])
                    last.then_inc(acc_free[s], 1)
                if st.nv == 2:
                    for s in range(RING):
                        v_tile(0, s)
                else:
                    with loop(0, st.nv // 2) as i:
                        for s in range(RING):
                            v_tile(i, s)

            def attend(st):
                scale = HD ** -0.5

                def bias(p):
                    c = p.c
                    if st.bias in ("alibi", "rpb"):
                        return bias_sb[:, p.tile_slot, :, c["bias"]:c["bias"] + p.n]
                    m = {"meta": meta_mask, "first": first_mask, "band": band_mask}[c["bias"]]
                    return m.unsqueeze(1).to_broadcast([p.nq, 2, p.n])

                def scores(p):
                    if p.b == 0 and st.bias == "alibi":
                        wait(alibi_full, 16 * p.tile + 16)
                    if p.b == 0 and st.bias == "rpb":
                        wait(rpb_masked, 2 * p.tile + 2)
                    if counted(2 * p.count - 2):
                        wait(pt_done, 2 * p.count - 2)
                    if st.sink is not None:
                        sink = sinks[st.sink][:, bass.ds(2 * p.tile, 2)].unsqueeze(2)
                        tt(s_sb[:, p.slot, :, 0:1], sink, sink, ALU.max)
                    wait(s_done, p.count + 1)
                    out = s_sb[0:p.nq, p.slot, :, 1:1 + p.n]
                    src = ps[0:p.nq, 2 * p.slot * BANK:2 * (p.slot + 1) * BANK]\
                        .rearrange("p (h n) -> p h n", h=2)[:, :, 0:p.n]
                    if st.bias is None:
                        ts(out, src, scale, None, ALU.mult).then_inc(s_read, 1)
                    else:
                        stt(out, src, scale, bias(p), ALU.mult, ALU.add).then_inc(s_read, 1)
                    off = 1 if st.sink is None else 0
                    reduce(n_max[0:p.nq, p.slot, :], s_sb[0:p.nq, p.slot, :, off:1 + p.n], AX.X, ALU.max,
                           negate=True).then_inc(max_ready, 1)

                def invert(p):
                    wait(p_ready, 2 * p.count + 2)
                    if counted(p.count - 1):
                        wait(rec_ready, p.count - 1)
                    recip(p_inv[0:p.nq, p.slot, :], p_sum[0:p.nq, p.slot, :]).then_inc(inv_ready, 1)

                def normalise(p):
                    wait(y_moved, p.count + 1)
                    y = y_sb[:, p.slot, 0:p.nq]
                    tt(y, y, bank(6 + p.slot)[:, P:P + p.nq], ALU.mult).then_inc(y_ready, 1)

                def step(p):
                    scores(p)
                    if p.back(1).exists:
                        invert(p.back(1))
                    if p.back(2).exists:
                        normalise(p.back(2))
                over_pairs(loop, st, step)
                last = last_pair(st)
                invert(last)
                normalise(last.back(1))
                normalise(last)

            def residual(q0, blk, squares):
                if squares:
                    clear_sum(squares)
                with loop(0, DT // 2) as i:
                    for s in range(RING):
                        ended(i + q0, s)
                        m = 2 * i + s
                        xm = halves_of(x[:, m, span(blk)], blk)
                        tt(xm, xm, acc(s, blk), ALU.add).then_inc(acc_free[s], 1)
                        if squares:
                            add_square(squares, m, s)

            def ffn(st):
                t = span(st.blk)
                if st.conv:
                    wait(h_ready, DT * st.nh0)
                    fill(padded[:, 0, 0:3], 0.0).then_inc(padded_zero, 1)
                for g in range(FF_G):
                    q0 = (st.slab0 + g * (2 * FF_J + DT)) // 2

                    def body(j):
                        done = j + st.ffn0 * FF_T + g * FF_J
                        if st.conv:
                            c0 = done - 2 * FF_T
                            layer = st.ffn0 - 2
                            wait(acc_free[0], j + q0 + 1)
                            w = [ffn_taps[:, layer, j + g * FF_J, k:k + 1] for k in range(3)]
                            ts(conv[:, 0, :], padded[:, 0, 3:3 + TOK], w[2], None, ALU.mult)\
                                .then_inc(tap_done, 1)
                            wait(tap_done, 2 * c0 + 1)
                            stt(conv[:, 0, :], padded[:, 0, 2:2 + TOK], w[1], conv[:, 0, :],
                                                           ALU.mult, ALU.add).then_inc(tap_done, 1)
                            wait(tap_done, 2 * c0 + 2)
                            stt(conv[:, 0, :], padded[:, 0, 1:1 + TOK], w[0], conv[:, 0, :],
                                                           ALU.mult, ALU.add).then_inc(conv_ready, 1)
                            wait(silu_ready, c0 + 1)
                        else:
                            wait(acc_free[0], j + q0 + 1)
                        ended(j + q0, 1)
                        tt(halves_of(prod[:, t], st.blk), halves_of(silu_g[:, t], st.blk),
                                                acc(1, st.blk), ALU.mult).then_inc(acc_free[1], 1)
                        wait(acc_free[1], j + q0 + 1)
                        copy(act_hi[:, j, t], prod[:, t]).then_inc(prod_ready, 1)
                        wait(prod_ready, done + 1)
                        tt(act_lo[:, j, t], prod[:, t], act_hi[:, j, t].bitcast(f32),
                                                ALU.subtract).then_inc(act_ready, 1)
                    wait(pe_done, 2 * q0)
                    if st.conv:
                        wait(padded_zero, st.ffn0 + 1)
                    with loop(0, FF_J) as j:
                        body(j)
                    residual(q0 + FF_J, st.blk, st.next_norm if g == FF_G - 1 else None)

            def taps(out, src, w, sem_, first):
                n = len(w)
                for j in range(n):
                    k = n - 1 - j
                    sh = slice(3 - j, 3 - j + TOK)
                    if j == 0:
                        ins = ts(out, src[:, sh], w[k], None, ALU.mult)
                    else:
                        wait(sem_, first + j)
                        ins = stt(out, src[:, sh], w[k], out, ALU.mult, ALU.add)
                    if j < n - 1:
                        ins.then_inc(sem_, 1)
                return ins

            def even(st):
                q0 = st.slab0 // 2
                wait(h_ready, DT * st.nh0)
                for s in range(RING):
                    fill(padded[:, s, 0:3], 0.0).then_inc(padded_zero, 1)
                copy(w_ba_hi[:, :, :], w_ba[:, :, :]).then_inc(ba_dve, 1)
                wait(ba_dve, 1)
                tt(w_ba_lo[:, :, :], w_ba[:, :, :], w_ba_hi[:, :, :].bitcast(f32), ALU.subtract)\
                    .then_inc(ba_dve, 1)
                wait(padded_zero, 2)
                with loop(0, 4) as i:
                    ended(i + q0, 0)
                    copy(halves_of(prod[:, :], 2), acc(0, 2)).then_inc(acc_free[0], 1)
                    wait(acc_free[0], i + q0 + 1)
                    ended(i + q0, 1)
                    tt(halves_of(padded[:, 0, 3:3 + TOK], 2), halves_of(prod[:, :], 2), acc(1, 2),
                                            ALU.mult).then_inc(acc_free[1], 1)
                    wait(acc_free[1], i + q0 + 1)
                    taps(conv_y[:, i, :], padded[:, 0, :], [a_taps[:, i, k:k + 1] for k in range(3)], ev_in, 2 * i)\
                        .then_inc(ev_tap, 1)
                wait(ev_tap, 4)
                with loop(0, 2) as i:
                    for s in range(RING):
                        ended(i + (q0 + 4), s)
                        v = halves_of(conv_y[:, 2 * i + s, :], 2)
                        tt(v, v, acc(s, 2), ALU.mult).then_inc(acc_free[s], 1)
                def conv_tile(i):
                    for s in range(RING):
                        ended(i + (q0 + 6), s)
                        copy(halves_of(padded[:, s, 3:3 + TOK], 2), acc(s, 2))\
                            .then_inc(acc_free[s], 1)
                        wait(acc_free[s], i + (q0 + 7))
                        if not isinstance(i, int):
                            wait(ev_silu, 2 * i + s - 1)
                        taps(conv[:, s, :], padded[:, s, :], [dn_taps[:, 2 * i + s, k:k + 1] for k in range(4)], ev_in,
                             6 * i + (8 + 3 * s)).then_inc(ev_conv, 1)
                peeled(loop, 6, conv_tile)
                fill(ba[:, :, :], 0.0).then_inc(ba_dve, 1)
                wait(ba_dve, 3)
                wait(ba_done, 1)
                copy(ba[0:META, 0, :], bank(4)[0:META, 0:8])
                copy(ba[:, 1:5, :], bank(4)[:, 8:40].rearrange("p (c n) -> p c n", n=8))\
                    .then_inc(head_step, 1)
                wait(head_step, 1)
                tt(dn_s[:, 0, :, :], ba[:, :, DN_H:8],
                                        dt_bias.unsqueeze(1).to_broadcast([P, 5, DN_H]), ALU.add).then_inc(head_step, 1)
                wait(head_step, 2)
                stt(dn_s[:, 2, :, :], dn_s[:, 0, :, :], -1.0, dn_s[:, 0, :, :], ALU.mult,
                                               ALU.min).then_inc(ba_dve, 1)
                wait(ba_act, 4)
                stt(dn_s[:, 3, :, :], dn_s[:, 0, :, :], 0.0, dn_s[:, 3, :, :], ALU.max,
                                               ALU.add).then_inc(head_step, 1)
                ts(dn_s[:, 1, :, :], dn_s[:, 1, :, :], 1.0, None, ALU.add).then_inc(head_step, 1)
                wait(head_step, 4)
                stt(gate[:, :, :], dn_s[:, 3, :, :], -1.0,
                                               ea[:, :].unsqueeze(1).to_broadcast([P, 5, DN_H]), ALU.mult, ALU.mult)\
                    .then_inc(head_step, 1)
                recip(beta[:, :, :], dn_s[:, 1, :, :]).then_inc(head_step, 1)
                wait(head_step, 6)

            def tile_norm(st):
                buf, segs, _ = tn_segments(st)
                done = st.tn0
                for start, n, gain in segs:
                    def body(i):
                        for s in range(RING):
                            j = 2 * i + s + done
                            wait(tn_r, j + 1)
                            tile = buf[:, 2 * i + s + start, :]
                            if st.what != "head":
                                stt(tile, tile, gain, root[:, s, :], ALU.mult, ALU.mult)\
                                    .then_inc(tn_out, 1)
                                continue
                            if counted(2 * i + s - 1):
                                wait(head_lo, 2 * i + s - 1)
                            stt(normed_o[:, s, :], tile, gain, root[:, s, :], ALU.mult, ALU.mult)\
                                .then_inc(tn_out, 1)
                            tt(normed_o[:, s, :], normed_o[:, s, :], zed[:, 2 * i + s, :],
                               ALU.mult).then_inc(head_ready, 1)
                    if st.what == "head":
                        peeled(loop, n // 2, body)
                    else:
                        with loop(0, n // 2) as i:
                            body(i)
                    done += n

            def delta():
                def chunk(c, n):
                    levels = delta_steps(n)[0]
                    t0 = 0 if isinstance(c, int) else P * c + (META - P)

                    def need(which, name):
                        wait((None, d_pe, d_dve, d_act, d_pool)[which], dn_at(which, c, name))

                    def per_token(v, m):
                        return v.unsqueeze(2).to_broadcast([v.shape[0], DN_H, m])

                    def all_heads(m):
                        return m[0:n, 0:n].unsqueeze(1).to_broadcast([n, DN_H, n])
                    sq4 = (slice(0, n), slice(None), slice(0, n))
                    if not isinstance(c, int):
                        wait(d_pe, dn_prev(1, c))
                        wait(d_act, dn_prev(3, c))
                        wait(d_dve, dn_prev(2, c))
                    tok = bass.ds(t0, n)
                    copy(kc[:, :, 0:n], qkv[:, 4:8, tok]).then_inc(d_dve, 1)
                    copy(vc[:, :, 0:n], qkv[:, 8:12, tok]).then_inc(d_dve, 1)
                    g_c, b_c = gate[:, c, :][0:n], beta[:, c, :][0:n]
                    copy(gb[0:n, :, :], per_token(g_c, P)).then_inc(d_dve, 1)
                    need(1, "rows")
                    copy(row[:, :, 0:n], quad(0, n)).then_inc(d_dve, 1)
                    copy(dcol[0:n, :], bank(1)[0:n, 0:DN_H]).then_inc(d_dve, 1)
                    need(2, "dcol")
                    tt(dlast[0:n, :], row[0:n, :, n - 1], dcol[0:n, :], ALU.subtract).then_inc(d_dve, 1)
                    tt(dt_[sq4], row[sq4], per_token(dcol[0:n, :], n), ALU.subtract).then_inc(d_dve, 1)
                    need(2, "dt")
                    tt(dt_[sq4], dt_[sq4], all_heads(after_eq), ALU.add).then_inc(d_dve, 1)
                    tt(dl_[sq4], per_token(dcol[0:n, :], n), row[sq4], ALU.subtract).then_inc(d_dve, 1)
                    need(2, "dl")
                    tt(dl_[sq4], dl_[sq4], all_heads(before), ALU.add).then_inc(d_dve, 1)
                    need(1, "kk")
                    need(3, "edl")
                    tt(a_m[sq4], quad(2, n)[0:n], dl_[sq4], ALU.mult).then_inc(d_dve, 1)
                    need(2, "a1")
                    tt(a_m[sq4], a_m[sq4], per_token(b_c, n), ALU.mult).then_inc(d_dve, 1)
                    need(1, "kq")
                    tt(qk_t[sq4], quad(3, n)[0:n], dt_[sq4], ALU.mult).then_inc(d_dve, 1)
                    need(1, "at")
                    copy(a_t[sq4], quad(1, n)[0:n]).then_inc(d_dve, 1)
                    tt(x_m[sq4], a_m[sq4], all_heads(first_level), ALU.mult).then_inc(d_dve, 1)
                    need(2, "x1")
                    tt(x_m[sq4], all_heads(ident), x_m[sq4], ALU.subtract).then_inc(d_dve, 1)
                    tt(x_t[sq4], a_t[sq4], all_heads(first_level_t), ALU.mult).then_inc(d_dve, 1)
                    need(2, "xt1")
                    tt(x_t[sq4], all_heads(ident), x_t[sq4], ALU.subtract).then_inc(d_dve, 1)
                    for s in levels:
                        if s != levels[-1]:
                            need(1, ("xx", s))
                            tt(x_m[sq4], x_m[sq4], quad(5, n)[0:n], ALU.subtract).then_inc(d_dve, 1)
                        need(1, ("xz", s))
                        tt(x_t[sq4], x_t[sq4], quad(6, n)[0:n], ALU.subtract).then_inc(d_dve, 1)
                    need(3, "elast")
                    tt(bed[0:n, :], b_c, edec[0:n, :], ALU.mult).then_inc(d_dve, 1)
                    need(2, "bed")
                    need(1, "kt")
                    tt(r1[0:n, :, :], quad(3, P)[0:n], per_token(bed[0:n, :], P), ALU.mult).then_inc(d_dve, 1)
                    tt(res[0:n, :, :], quad(7, P)[0:n], per_token(b_c, P), ALU.mult).then_inc(d_dve, 1)
                    need(2, "r2")
                    tt(res[0:n, :, :], res[0:n, :, :], r1[0:n, :, :], ALU.subtract).then_inc(d_dve, 1)
                    tt(k_dec[0:n, :, :], quad(2, P)[0:n], per_token(elast[0:n, :], P), ALU.mult).then_inc(d_dve, 1)
                    tt(q_dec[:, :, 0:n], qkv[:, 0:4, tok], erow[:, :, 0:n], ALU.mult).then_inc(d_dve, 1)
                    need(1, "o")
                    tt(state[:, :, :], state[:, :, :], per_token(erow[:, :, n - 1], P), ALU.mult).then_inc(d_dve, 1)
                    need(2, "s1")
                    need(1, "s")
                    tt(state[:, :, :], state[:, :, :], quad(4, P), ALU.add).then_inc(d_dve, 1)
                    copy(qkv[:, 8:12, tok], quad(6, n)).then_inc(d_dve, 1)
                wait(tn_out, 8)
                wait(loaded, 16 * N_LOADS + 16)
                fill(state[:, :, :], 0.0)
                chunk(0, META)
                with loop(1, 5) as c:
                    chunk(c, P)

            wait(mem_loaded, 16 * N_FIRST)
            for n, st in enumerate(stages):
                if st.kind == "norm":
                    if n == 2:
                        wait(loaded, 16 * N_LOADS)
                    norm(st)
                elif st.kind == "memkv":
                    memkv(st)
                elif st.kind == "proj":
                    proj(st)
                elif st.kind == "att":
                    attend(st)
                elif st.kind == "out":
                    residual(st.slab0 // 2, st.blk, st.next_norm)
                elif st.kind == "ffn":
                    ffn(st)
                elif st.kind == "even":
                    even(st)
                elif st.kind == "tn":
                    tile_norm(st)
                elif st.kind == "delta":
                    delta()


def constants():
    import numpy as np
    p, c = np.arange(P)[:, None], np.arange(P)[None, :]
    zero = lambda ok: np.where(ok, 0.0, NEG)
    parts = [zero(c >= p), zero(p > c)]
    for s in range(1, LEVELS):
        parts.append((p >> (s + 1) == c >> (s + 1)) & ((p >> s) & 1 == 0) & ((c >> s) & 1 == 1))
    parts.append((p >> 1 == c >> 1) & (p % 2 == 1) & (c % 2 == 0))
    parts.append((p >> 1 == c >> 1) & (p % 2 == 0) & (c % 2 == 1))
    dn_consts = np.concatenate([np.asarray(a, np.float32) for a in parts], axis=1)
    parts = [p == c, np.ones((P, P)), p // HD == c // HD, p <= c]
    col = np.arange(GRID)
    start = np.clip(col - 8, 0, GRID - 16)
    inside = (col[None, :] >= start[:, None]) & (col[None, :] < start[:, None] + 16)
    parts.append(zero(np.tile(inside, (2, 1))))
    prev, cur = zero(c > p), zero(c <= p)
    meta = np.zeros((P, META))
    parts += [prev, meta, cur, cur, meta, zero(np.arange(META)[None, :] <= p)]
    consts = np.concatenate([np.asarray(a, np.float32) for a in parts], axis=1)
    dist = np.abs(np.arange(P)[:, None] + P - np.arange(3 * P)[None, :])
    slopes = np.float32(2.0) ** (np.float32(-8.0) * np.arange(1, 13, dtype=np.float32) / np.float32(12))
    order = [h for pair in L0_PAIRS for h in pair]
    alibi = np.where(dist <= P, -slopes[order][:, None, None] * dist.astype(np.float32), np.float32(NEG))
    return consts, dn_consts, alibi.reshape(6, 2, P, 3 * P).astype(np.float32)


def kernel(x, mem, norm_mix, norm_ffn, norm_mem, norm_final, w_in_a, sink_a, w_in_b, rpb_b, w_mem_kv, w_out,
           w_gate_up, w_down, meta_tokens_2, attn_norm_w_2, ffn_norm_w_2, mix_w_in_2, conv_a_w_2, dn_conv_w_2,
           dn_a_log_2, dn_dt_bias_2, dn_norm_w_2, mix_w_out_2, swa_wq_2, swa_wk_2, swa_wv_2, swa_q_norm_w_2,
           swa_k_norm_w_2, swa_sinks_2, swa_wo_2, ffn_w_up_2, ffn_conv_w_2, ffn_w_down_2):
    import numpy as np
    import concourse.bacc as bacc
    from concourse.bass_utils import run_bass_kernel_spmd

    def rows_of(w, order):
        n = len(order) * HD
        return np.concatenate([w[:n].reshape(-1, HD, w.shape[1])[order].reshape(n, -1), w[n:]])

    def cols_of(w, order):
        return w.reshape(w.shape[0], -1, HD)[:, order].reshape(w.shape[0], -1)

    def slabs_of(w):
        return w.reshape(DT, P, -1, P).transpose(2, 1, 0, 3).reshape(-1, P, DT * P)

    def ffn_slabs(up, down):
        gate, val = slabs_of(up[:, :FF_T * P]), slabs_of(up[:, FF_T * P:])
        both = np.stack([gate, val], 1).reshape(FF_G, 2 * FF_J, P, DT * P)
        dn = down.reshape(FF_G, FF_J, P, DT, P).transpose(0, 3, 2, 1, 4).reshape(FF_G, DT, P, DOWN * P)
        return both, dn

    order0 = [h for pair in L0_PAIRS for h in pair]
    order3 = [h for pair in L3_PAIRS for h in pair]
    eight, eleven = [], []
    for layer in range(2):
        eight.append(slabs_of(w_mem_kv[layer]))

    def tail(w_o, up, down):
        eight.append(slabs_of(w_o))
        both, dn = ffn_slabs(up, down)
        for g in range(FF_G):
            eight.append(both[g])
            eleven.append(dn[g])

    wa, wb = w_in_a[0], w_in_b[0]
    eight += [slabs_of(cols_of(wa[:, :768], order0)), slabs_of(wa[:, 768:1024]), slabs_of(wa[:, 1280:]),
              slabs_of(wa[:, 1024:1280])]
    tail(rows_of(w_out[0], order0), w_gate_up[0], w_down[0])
    eight += [slabs_of(wb[:, :1536]), slabs_of(wb[:, 2304:]), slabs_of(wb[:, 1536:2304])]
    tail(w_out[1], w_gate_up[1], w_down[1])
    wm = mix_w_in_2[0]
    pairs = np.stack([slabs_of(wm[:, :512]), slabs_of(wm[:, 1024:1536])], 1).reshape(8, P, DT * P)
    eight += [pairs, slabs_of(wm[:, 512:1024]), slabs_of(wm[:, 1536:3584])]
    tail(mix_w_out_2[0], ffn_w_up_2[0], ffn_w_down_2[0])
    eight += [slabs_of(cols_of(swa_wq_2[0], order3)), slabs_of(swa_wk_2[0]), slabs_of(swa_wv_2[0])]
    tail(rows_of(swa_wo_2[0], order3), ffn_w_up_2[1], ffn_w_down_2[1])

    consts, dn_consts, alibi = constants()
    gains = [norm_mem, norm_mix[0], norm_ffn[0], norm_mix[1], norm_ffn[1], norm_final, attn_norm_w_2[0],
             ffn_norm_w_2[0], attn_norm_w_2[1], ffn_norm_w_2[1]]

    def per_feature(a):
        return a.reshape(-1, P, a.shape[1]).transpose(1, 0, 2).reshape(P, -1)

    two = lambda w: np.concatenate([w, w])[:, None]
    vectors = np.concatenate(
        [per_feature(np.asarray(g)[:, None]) for g in gains]
        + [per_feature(np.asarray(w).T) for w in (*ffn_conv_w_2, conv_a_w_2[0], dn_conv_w_2[0])]
        + [np.asarray(dn_norm_w_2[0])[:, None], two(swa_q_norm_w_2[0]), two(swa_k_norm_w_2[0]),
           np.full((P, 1), EPS, np.float32)], axis=1)
    rpb = np.pad(rpb_b[0][:, :, ::-1], ((0, 0), (0, 0), (GRID - 16, GRID - 16)))
    arrays = {
        "x": x[0].T, "mem": mem[0].T, "meta": meta_tokens_2.T,
        "slabs8": np.concatenate(eight), "slabs11": np.concatenate(eleven),
        "consts": consts, "dn_consts": dn_consts, "alibi": alibi, "vectors": vectors, "rpb": rpb,
        "sink_a": sink_a[0][order0], "sink_b": swa_sinks_2[0][order3],
        "dn_rows": np.concatenate([dn_a_log_2[0], dn_dt_bias_2[0]]), "w_ba": wm[:, 3584:],
    }
    nc = bacc.Bacc("TRN2", target_bir_lowering=False, num_devices=1)
    f32 = mybir.dt.float32
    arrays = {k: np.ascontiguousarray(v) for k, v in arrays.items()}
    dram = {k: nc.dram_tensor(k + "_d", v.shape, f32, kind="ExternalInput").ap() for k, v in arrays.items()}
    dram["alibi"] = dram["alibi"].rearrange("i h p k -> i p h k")
    dram["out"] = nc.dram_tensor("out_d", (D, SEQ), f32, kind="ExternalOutput").ap()
    build(nc, dram)
    r = run_bass_kernel_spmd(nc, [{k + "_d": v for k, v in arrays.items()}], core_ids=[0])
    return r.results[0]["out_d"].T[None]
```
